# Optimizing a Trainium2 kernel written in Bass

```python
import jax, jax.numpy as jnp
from jax import lax
import numpy as np
import math
import jax
import jax.numpy as jnp

D_MODEL = 1024
BATCH = 1
SEQ = 256
DEPTH = 2

GRID_W = 64
WIN_H_MAX = 8
WIN_W = 16
COL_BLOCK = 16
COL_SLAB = 32
NA_HEADS = 8
NA_HEAD_DIM = 64
NA_WIDTH = NA_HEADS * NA_HEAD_DIM
GLA_HEADS = 4
GLA_DK = 64
GLA_DV = 128
GLA_QK_WIDTH = GLA_HEADS * GLA_DK
GLA_V_WIDTH = GLA_HEADS * GLA_DV
GLA_GATE_RANK = 16
GLA_TAU = 16.0
GLA_CHUNK = 64
MIX_WIDTH = NA_WIDTH + GLA_V_WIDTH
IN_SPLITS = (NA_WIDTH, NA_WIDTH, NA_WIDTH,
             GLA_QK_WIDTH, GLA_QK_WIDTH,
             GLA_V_WIDTH, GLA_V_WIDTH,
             GLA_GATE_RANK, GLA_GATE_RANK)
IN_WIDTH = sum(IN_SPLITS)
D_FF = 2816
EPS = 1e-6
NEG_INF = -1e30


def rmsnorm(x, g):
    xf = x.astype(jnp.float32)
    y = xf * lax.rsqrt(jnp.mean(xf * xf, axis=-1, keepdims=True) + EPS)
    return (y * g.astype(jnp.float32)).astype(x.dtype)

def swiglu(h, w_gate, w_up, w_down):
    return (jax.nn.silu(h @ w_gate) * (h @ w_up)) @ w_down

def split_heads(a, n):
    b, s, w = a.shape
    return a.reshape(b, s, n, w // n).transpose(0, 2, 1, 3)

def merge_heads(a):
    b, n, s, d = a.shape
    return a.transpose(0, 2, 1, 3).reshape(b, s, n * d)

def neighbourhood_attention(q, k, v, rpb):
    B, H, S, d = q.shape
    rows = S // GRID_W
    wh = min(WIN_H_MAX, rows)
    q = q.reshape(B, H, rows, GRID_W, d)
    k = k.reshape(B, H, rows, GRID_W, d)
    v = v.reshape(B, H, rows, GRID_W, d)
    r = np.arange(rows)
    row_start = np.clip(r - wh // 2, 0, rows - wh)
    key_rows = row_start[:, None] + np.arange(wh)[None, :]
    dr = key_rows - r[:, None] + (WIN_H_MAX - 1)
    scale = NA_HEAD_DIM ** -0.5
    outs = []
    for j in range(GRID_W // COL_BLOCK):
        qc = np.arange(j * COL_BLOCK, (j + 1) * COL_BLOCK)
        col_start = np.clip(qc - WIN_W // 2, 0, GRID_W - WIN_W)
        c0 = int(np.clip(j * COL_BLOCK - WIN_W // 2, 0, GRID_W - COL_SLAB))
        kc = c0 + np.arange(COL_SLAB)
        valid = (kc[None, :] >= col_start[:, None]) & (kc[None, :] < col_start[:, None] + WIN_W)
        dc = np.clip(kc[None, :] - qc[:, None] + (WIN_W - 1), 0, 2 * WIN_W - 2)
        qb = q[:, :, :, j * COL_BLOCK:(j + 1) * COL_BLOCK]
        kb = k[:, :, :, c0:c0 + COL_SLAB][:, :, key_rows]
        vb = v[:, :, :, c0:c0 + COL_SLAB][:, :, key_rows]
        s = jnp.einsum('bhrqd,bhrwkd->bhrqwk', qb, kb).astype(jnp.float32) * scale
        bias = rpb[:, dr[:, None, :, None], dc[None, :, None, :]]
        s = s + bias[None].astype(jnp.float32)
        s = jnp.where(valid[:, None, :], s, NEG_INF)
        p = jax.nn.softmax(s.reshape(B, H, rows, COL_BLOCK, wh * COL_SLAB), axis=-1)
        p = p.reshape(B, H, rows, COL_BLOCK, wh, COL_SLAB).astype(v.dtype)
        outs.append(jnp.einsum('bhrqwk,bhrwkd->bhrqd', p, vb))
    o = jnp.concatenate(outs, axis=3)
    return o.reshape(B, H, S, d)

def gla_chunked(q, k, v, g, include_diag):
    B, H, T, dk = q.shape
    dv = v.shape[-1]
    n = T // GLA_CHUNK

    def to_chunks(a):
        return jnp.moveaxis(a.reshape(B, H, n, GLA_CHUNK, a.shape[-1]), 2, 0)

    t = np.arange(GLA_CHUNK)
    mask = (t[:, None] >= t[None, :]) if include_diag else (t[:, None] > t[None, :])

    def step(state, inp):
        qi, ki, vi, gi = inp
        b = jnp.cumsum(gi, axis=-2)
        inter = jnp.einsum('bhtd,bhde->bhte', qi * jnp.exp(b), state)
        diff = b[:, :, :, None, :] - b[:, :, None, :, :]
        decay = jnp.exp(jnp.where(mask[:, :, None], diff, -jnp.inf))
        a = jnp.einsum('bhtd,bhsd,bhtsd->bhts', qi, ki, decay)
        intra = jnp.einsum('bhts,bhse->bhte', a, vi)
        b_last = b[:, :, -1:, :]
        state = (jnp.exp(b_last[:, :, 0, :])[..., None] * state
                 + jnp.einsum('bhsd,bhse->bhde', ki * jnp.exp(b_last - b), vi))
        return state, inter + intra

    s0 = jnp.zeros((B, H, dk, dv), jnp.float32)
    _, o = lax.scan(step, s0, (to_chunks(q), to_chunks(k), to_chunks(v), to_chunks(g)))
    return jnp.moveaxis(o, 0, 2).reshape(B, H, T, dv)

def hybrid_layer(x, ffn1_norm, ffn1_wg, ffn1_wu, ffn1_wd, mix_norm, w_in, na_rpb, na_gain,
                 w_gate_f, b_gate_f, w_gate_b, b_gate_b, gla_gain, w_out,
                 ffn2_norm, ffn2_wg, ffn2_wu, ffn2_wd):
    x = x + 0.5 * swiglu(rmsnorm(x, ffn1_norm), ffn1_wg, ffn1_wu, ffn1_wd)

    h = rmsnorm(x, mix_norm)
    proj = h @ w_in
    offsets = list(np.cumsum(IN_SPLITS)[:-1])
    na_q, na_k, na_v, g_q, g_k, g_v, g_r, gf_code, gb_code = jnp.split(proj, offsets, axis=-1)

    na_o = neighbourhood_attention(split_heads(na_q, NA_HEADS), split_heads(na_k, NA_HEADS),
                                   split_heads(na_v, NA_HEADS), na_rpb)
    na_o = rmsnorm(merge_heads(na_o), na_gain)

    f32 = jnp.float32
    qg = split_heads(g_q, GLA_HEADS).astype(f32) * (GLA_DK ** -0.5)
    kg = split_heads(g_k, GLA_HEADS).astype(f32)
    vg = split_heads(g_v, GLA_HEADS).astype(f32)
    log_gf = jax.nn.log_sigmoid((gf_code @ w_gate_f + b_gate_f).astype(f32)) / GLA_TAU
    log_gb = jax.nn.log_sigmoid((gb_code @ w_gate_b + b_gate_b).astype(f32)) / GLA_TAU
    log_gf = split_heads(log_gf, GLA_HEADS)
    log_gb = split_heads(log_gb, GLA_HEADS)
    o_fwd = gla_chunked(qg, kg, vg, log_gf, True)
    flip = lambda a: jnp.flip(a, axis=2)
    o_bwd = flip(gla_chunked(flip(qg), flip(kg), flip(vg), flip(log_gb), False))
    gla_o = rmsnorm(o_fwd + o_bwd, gla_gain).astype(x.dtype)
    gla_o = merge_heads(gla_o) * jax.nn.silu(g_r)

    x = x + jnp.concatenate([na_o, gla_o], axis=-1) @ w_out

    x = x + 0.5 * swiglu(rmsnorm(x, ffn2_norm), ffn2_wg, ffn2_wu, ffn2_wd)
    return x

def first_inputs(seed: int = 0) -> dict:
    key = jax.random.key(seed)
    ks = iter(jax.random.split(key, 32))
    nrm = lambda shape, s: jax.random.normal(next(ks), shape, jnp.float32) * s
    gain = lambda shape: 1.0 + nrm(shape, 0.02)
    L, D = DEPTH, D_MODEL
    return {
        "x": nrm((BATCH, SEQ, D), 1.0),
        "ffn1_norm": gain((L, D)),
        "ffn1_wg": nrm((L, D, D_FF), D ** -0.5),
        "ffn1_wu": nrm((L, D, D_FF), D ** -0.5),
        "ffn1_wd": nrm((L, D_FF, D), D_FF ** -0.5),
        "mix_norm": gain((L, D)),
        "w_in": nrm((L, D, IN_WIDTH), D ** -0.5),
        "na_rpb": nrm((L, NA_HEADS, 2 * WIN_H_MAX - 1, 2 * WIN_W - 1), 0.1),
        "na_gain": gain((L, NA_WIDTH)),
        "w_gate_f": nrm((L, GLA_GATE_RANK, GLA_QK_WIDTH), GLA_GATE_RANK ** -0.5),
        "b_gate_f": nrm((L, GLA_QK_WIDTH), 0.1),
        "w_gate_b": nrm((L, GLA_GATE_RANK, GLA_QK_WIDTH), GLA_GATE_RANK ** -0.5),
        "b_gate_b": nrm((L, GLA_QK_WIDTH), 0.1),
        "gla_gain": gain((L, GLA_DV)),
        "w_out": nrm((L, MIX_WIDTH, D), MIX_WIDTH ** -0.5),
        "ffn2_norm": gain((L, D)),
        "ffn2_wg": nrm((L, D, D_FF), D ** -0.5),
        "ffn2_wu": nrm((L, D, D_FF), D ** -0.5),
        "ffn2_wd": nrm((L, D_FF, D), D_FF ** -0.5),
        "final_norm": gain((D,)),
    }

def first_block(x, ffn1_norm, ffn1_wg, ffn1_wu, ffn1_wd, mix_norm, w_in, na_rpb, na_gain,
              w_gate_f, b_gate_f, w_gate_b, b_gate_b, gla_gain, w_out,
              ffn2_norm, ffn2_wg, ffn2_wu, ffn2_wd, final_norm):
    for l in range(DEPTH):
        x = hybrid_layer(x, ffn1_norm[l], ffn1_wg[l], ffn1_wu[l], ffn1_wd[l], mix_norm[l], w_in[l],
                         na_rpb[l], na_gain[l], w_gate_f[l], b_gate_f[l], w_gate_b[l], b_gate_b[l],
                         gla_gain[l], w_out[l], ffn2_norm[l], ffn2_wg[l], ffn2_wu[l], ffn2_wd[l])
    return rmsnorm(x, final_norm)


D_MIX = D_MODEL
HEAD_DIM = 64
FOX_WIDTH = D_MIX // 4
DIL_WIDTH = D_MIX // 4
HGRN_WIDTH = D_MIX // 2
FOX_HEADS = FOX_WIDTH // HEAD_DIM
DIL_HEADS = DIL_WIDTH // HEAD_DIM
HGRN_EXPAND = 128
HGRN_HEADS = HGRN_WIDTH // HGRN_EXPAND
HGRN_VDIM = HGRN_WIDTH // HGRN_HEADS
HGRN_FDIM = HGRN_HEADS * HGRN_EXPAND
HGRN_CHUNK = 64
Q_BLOCK = 128
DILATED_PATTERNS = ((128, 1), (512, 4), (2048, 16))
ROPE_DIM = HEAD_DIM // 4
ROPE_THETA = 500000.0
D_FF_2 = ((8 * D_MODEL // 3 + 127) // 128) * 128
NEG_BIG = -1e30
LB_FLOOR = 1e-30

SPLIT_SIZES = (FOX_WIDTH, FOX_WIDTH, FOX_WIDTH, FOX_HEADS,
               DIL_WIDTH, DIL_WIDTH, DIL_WIDTH,
               HGRN_FDIM, HGRN_FDIM, HGRN_WIDTH, HGRN_WIDTH)
N_IN = sum(SPLIT_SIZES)
SPLIT_POINTS = tuple(int(s) for s in np.cumsum(SPLIT_SIZES)[:-1])


def _rmsnorm(x, g):
    xf = x.astype(jnp.float32)
    y = xf * lax.rsqrt(jnp.mean(xf * xf, axis=-1, keepdims=True) + EPS)
    return (y * g.astype(jnp.float32)).astype(x.dtype)

def _swiglu(h, wg, wu, wd):
    return (jax.nn.silu(h @ wg) * (h @ wu)) @ wd

def _partial_rope(t, positions):
    half = ROPE_DIM // 2
    freqs = ROPE_THETA ** (-jnp.arange(0, ROPE_DIM, 2, dtype=jnp.float32) / ROPE_DIM)
    ang = positions.astype(jnp.float32)[:, :, None] * freqs
    cos = jnp.cos(ang)[:, :, None, :]
    sin = jnp.sin(ang)[:, :, None, :]
    tf = t.astype(jnp.float32)
    x1, x2, rest = tf[..., :half], tf[..., half:ROPE_DIM], tf[..., ROPE_DIM:]
    out = jnp.concatenate([x1 * cos - x2 * sin, x2 * cos + x1 * sin, rest], axis=-1)
    return out.astype(t.dtype)

def _fox_attention(q, k, v, c):
    B, H, T, dh = q.shape
    nb = T // Q_BLOCK
    scale = dh ** -0.5
    qb = q.reshape(B, H, nb, Q_BLOCK, dh).transpose(2, 0, 1, 3, 4)
    cb = c.reshape(B, H, nb, Q_BLOCK).transpose(2, 0, 1, 3)
    kpos = jnp.arange(T)

    def block(args):
        qi, ci, n = args
        s = jnp.einsum('bhqd,bhkd->bhqk', qi, k).astype(jnp.float32) * scale
        s = s + ci[..., None] - c[:, :, None, :]
        qpos = n * Q_BLOCK + jnp.arange(Q_BLOCK)
        mask = kpos[None, :] <= qpos[:, None]
        p = jax.nn.softmax(jnp.where(mask, s, NEG_BIG), axis=-1)
        return jnp.einsum('bhqk,bhkd->bhqd', p.astype(v.dtype), v)

    out = lax.map(block, (qb, cb, jnp.arange(nb)))
    return out.transpose(1, 2, 0, 3, 4).reshape(B, H, T, dh)

def _dilated_branch(q, k, v, window, dilation):
    B, H, T, dh = q.shape
    L = T // dilation
    w = window // dilation
    blk = min(w, L)
    nb = -(-L // blk)
    Lp = nb * blk
    scale = dh ** -0.5

    def to_blocks(t):
        t = t.reshape(B, H, L, dilation, dh).transpose(0, 1, 3, 2, 4)
        t = jnp.pad(t, ((0, 0), (0, 0), (0, 0), (0, Lp - L), (0, 0)))
        return t.reshape(B, H, dilation, nb, blk, dh)

    def with_prev(t):
        prev = jnp.pad(t, ((0, 0), (0, 0), (0, 0), (1, 0), (0, 0), (0, 0)))[:, :, :, :nb]
        return jnp.concatenate([prev, t], axis=4)

    qb = to_blocks(q)
    kc = with_prev(to_blocks(k))
    vc = with_prev(to_blocks(v))
    s = jnp.einsum('bhrnqd,bhrnkd->bhrnqk', qb, kc).astype(jnp.float32) * scale
    i = jnp.arange(blk)[:, None]
    j = jnp.arange(2 * blk)[None, :]
    rel = blk + i - j
    first = (jnp.arange(nb)[:, None, None] == 0) & (j < blk)[None]
    mask = ((rel >= 0) & (rel <= w))[None] & ~first
    s = jnp.where(mask, s, NEG_BIG)
    m = jnp.max(s, axis=-1, keepdims=True)
    p = jnp.exp(s - m)
    den = jnp.sum(p, axis=-1)
    o = jnp.einsum('bhrnqk,bhrnkd->bhrnqd', p, vc.astype(jnp.float32)) / den[..., None]
    lse = m[..., 0] + jnp.log(den)
    o = o.reshape(B, H, dilation, Lp, dh)[:, :, :, :L].transpose(0, 1, 3, 2, 4).reshape(B, H, T, dh)
    lse = lse.reshape(B, H, dilation, Lp)[..., :L].transpose(0, 1, 3, 2).reshape(B, H, T)
    return o, lse

def _dilated_attention(q, k, v):
    outs, lses = [], []
    for window, dilation in DILATED_PATTERNS:
        o, lse = _dilated_branch(q, k, v, window, dilation)
        outs.append(o)
        lses.append(lse)
    wts = jax.nn.softmax(jnp.stack(lses, 0), axis=0)
    return jnp.sum(wts[..., None] * jnp.stack(outs, 0), axis=0)

def _hgrn2(q_raw, f_raw, i_raw, g_raw, lb, norm_w):
    B, T, _ = q_raw.shape
    H, E, V, C = HGRN_HEADS, HGRN_EXPAND, HGRN_VDIM, HGRN_CHUNK
    nc = T // C
    lbf = jnp.clip(lb.astype(jnp.float32), 0.0, 1.0 - 1e-6)
    z = f_raw.astype(jnp.float32)
    log_f = jnp.logaddexp(jnp.log(jnp.maximum(lbf, LB_FLOOR)),
                          jnp.log1p(-lbf) + jax.nn.log_sigmoid(z))
    kk = (1.0 - lbf) * jax.nn.sigmoid(-z)
    qq = jax.nn.silu(q_raw.astype(jnp.float32))
    vv = i_raw.astype(jnp.float32)

    def chunks(t, d):
        return t.reshape(B, nc, C, H, d).transpose(1, 0, 3, 2, 4)

    causal = jnp.arange(C)[:, None] >= jnp.arange(C)[None, :]

    def step(S, inp):
        q, k, v, lf = inp
        b = jnp.cumsum(lf, axis=2)
        inter = jnp.einsum('bhte,bhev->bhtv', q * jnp.exp(b), S)
        diff = b[:, :, :, None, :] - b[:, :, None, :, :]
        D = jnp.exp(jnp.where(causal[None, None, :, :, None], diff, NEG_BIG))
        A = jnp.einsum('bhtse,bhse->bhts', q[:, :, :, None, :] * D, k)
        intra = jnp.einsum('bhts,bhsv->bhtv', A, v)
        b_last = b[:, :, -1, :]
        S_new = jnp.exp(b_last)[..., None] * S + jnp.einsum(
            'bhse,bhsv->bhev', k * jnp.exp(b_last[:, :, None, :] - b), v)
        return S_new, inter + intra

    S0 = jnp.zeros((B, H, E, V), jnp.float32)
    _, o = lax.scan(step, S0, (chunks(qq, E), chunks(kk, E), chunks(vv, V), chunks(log_f, E)))
    o = o.transpose(1, 0, 3, 2, 4).reshape(B, T, H, V)
    o = o * lax.rsqrt(jnp.mean(o * o, axis=-1, keepdims=True) + EPS)
    o = o.reshape(B, T, H * V) * norm_w.astype(jnp.float32)
    return o * jax.nn.sigmoid(g_raw.astype(jnp.float32))

def _mixing(h, positions, w_in, w_out, fox_b, lb, hgrn_norm):
    B, T, _ = h.shape
    proj = h @ w_in
    (fq, fk, fv, ff, dq, dk, dv, hq, hf, hi, hg) = jnp.split(proj, SPLIT_POINTS, axis=-1)

    def heads(t, n):
        return t.reshape(B, T, n, HEAD_DIM)

    log_fg = jax.nn.log_sigmoid((ff + fox_b).astype(jnp.float32))
    c = jnp.cumsum(log_fg, axis=1).transpose(0, 2, 1)
    tr = lambda t: t.transpose(0, 2, 1, 3)
    oa = _fox_attention(tr(heads(fq, FOX_HEADS)), tr(heads(fk, FOX_HEADS)),
                        tr(heads(fv, FOX_HEADS)), c)
    oa = oa.transpose(0, 2, 1, 3).reshape(B, T, FOX_WIDTH)

    qd = _partial_rope(heads(dq, DIL_HEADS), positions)
    kd = _partial_rope(heads(dk, DIL_HEADS), positions)
    ob = _dilated_attention(tr(qd), tr(kd), tr(heads(dv, DIL_HEADS)))
    ob = ob.transpose(0, 2, 1, 3).reshape(B, T, DIL_WIDTH)

    oc = _hgrn2(hq, hf, hi, hg, lb, hgrn_norm)

    o = jnp.concatenate([oa.astype(h.dtype), ob.astype(h.dtype), oc.astype(h.dtype)], axis=-1)
    return o @ w_out

def second_inputs(seed: int = 0) -> dict:
    key = jax.random.key(seed)
    ks = jax.random.split(key, 20)
    f32 = jnp.float32
    nrm = lambda k, shape, fan: jax.random.normal(k, shape, f32) * fan ** -0.5
    gain = lambda k, shape: 1.0 + 0.02 * jax.random.normal(k, shape, f32)
    x = jax.random.normal(ks[0], (BATCH, SEQ, D_MODEL), f32)
    positions = jnp.broadcast_to(jnp.arange(SEQ, dtype=jnp.int32)[None, :], (BATCH, SEQ))
    return {
        "x": x,
        "positions": positions,
        "ffn1_norm": gain(ks[1], (DEPTH, D_MODEL)),
        "ffn1_w_gate": nrm(ks[2], (DEPTH, D_MODEL, D_FF_2), D_MODEL),
        "ffn1_w_up": nrm(ks[3], (DEPTH, D_MODEL, D_FF_2), D_MODEL),
        "ffn1_w_down": nrm(ks[4], (DEPTH, D_FF_2, D_MODEL), D_FF_2),
        "mix_norm": gain(ks[5], (DEPTH, D_MODEL)),
        "w_in": nrm(ks[6], (DEPTH, D_MODEL, N_IN), D_MODEL),
        "fox_forget_bias": 2.0 + 0.5 * jax.random.normal(ks[7], (DEPTH, FOX_HEADS), f32),
        "hgrn_lower_bounds": 0.1 * jax.random.normal(ks[8], (DEPTH, HGRN_FDIM), f32),
        "hgrn_out_norm": gain(ks[9], (DEPTH, HGRN_WIDTH)),
        "w_out": nrm(ks[10], (DEPTH, D_MIX, D_MODEL), D_MIX),
        "ffn2_norm": gain(ks[11], (DEPTH, D_MODEL)),
        "ffn2_w_gate": nrm(ks[12], (DEPTH, D_MODEL, D_FF_2), D_MODEL),
        "ffn2_w_up": nrm(ks[13], (DEPTH, D_MODEL, D_FF_2), D_MODEL),
        "ffn2_w_down": nrm(ks[14], (DEPTH, D_FF_2, D_MODEL), D_FF_2),
        "final_norm": gain(ks[15], (D_MODEL,)),
    }

def second_block(x, positions, ffn1_norm, ffn1_w_gate, ffn1_w_up, ffn1_w_down, mix_norm, w_in,
              fox_forget_bias, hgrn_lower_bounds, hgrn_out_norm, w_out, ffn2_norm,
              ffn2_w_gate, ffn2_w_up, ffn2_w_down, final_norm):
    sm = jax.nn.softmax(hgrn_lower_bounds.astype(jnp.float32), axis=0)
    lbs = jnp.cumsum(sm, axis=0) - sm[0:1]
    for i in range(DEPTH):
        h = _rmsnorm(x, ffn1_norm[i])
        x = x + 0.5 * _swiglu(h, ffn1_w_gate[i], ffn1_w_up[i], ffn1_w_down[i])
        h = _rmsnorm(x, mix_norm[i])
        x = x + _mixing(h, positions, w_in[i], w_out[i], fox_forget_bias[i], lbs[i],
                        hgrn_out_norm[i])
        h = _rmsnorm(x, ffn2_norm[i])
        x = x + 0.5 * _swiglu(h, ffn2_w_gate[i], ffn2_w_up[i], ffn2_w_down[i])
    return _rmsnorm(x, final_norm)


def setup_inputs(seed=0):
    out = dict(first_inputs(seed))
    for name, value in second_inputs(seed + 1).items():
        if name != "x":
            out[name + "_2"] = value
    return out


def reference(
    x, ffn1_norm, ffn1_wg, ffn1_wu, ffn1_wd, mix_norm, w_in, na_rpb, na_gain, w_gate_f,
    b_gate_f, w_gate_b, b_gate_b, gla_gain, w_out, ffn2_norm, ffn2_wg, ffn2_wu, ffn2_wd,
    final_norm, positions_2, ffn1_norm_2, ffn1_w_gate_2, ffn1_w_up_2, ffn1_w_down_2, mix_norm_2,
    w_in_2, fox_forget_bias_2, hgrn_lower_bounds_2, hgrn_out_norm_2, w_out_2, ffn2_norm_2,
    ffn2_w_gate_2, ffn2_w_up_2, ffn2_w_down_2, final_norm_2,
):
    x = first_block(
        x, ffn1_norm, ffn1_wg, ffn1_wu, ffn1_wd, mix_norm, w_in, na_rpb, na_gain, w_gate_f,
        b_gate_f, w_gate_b, b_gate_b, gla_gain, w_out, ffn2_norm, ffn2_wg, ffn2_wu, ffn2_wd,
        final_norm,
    )
    return second_block(
        x, positions_2, ffn1_norm_2, ffn1_w_gate_2, ffn1_w_up_2, ffn1_w_down_2, mix_norm_2,
        w_in_2, fox_forget_bias_2, hgrn_lower_bounds_2, hgrn_out_norm_2, w_out_2, ffn2_norm_2,
        ffn2_w_gate_2, ffn2_w_up_2, ffn2_w_down_2, final_norm_2,
    )


_drawn_inputs = setup_inputs


def setup_inputs(seed=0):
    import zlib

    import numpy as np

    out = dict(_drawn_inputs(seed))
    spreads = {}
    factors = {'ffn1_norm': 3.252,
     'na_gain': 2.78,
     'b_gate_f': 3.546,
     'b_gate_b': 3.711,
     'gla_gain': 5.325,
     'ffn2_norm': 5.462,
     'ffn1_norm_2': 4.959,
     'mix_norm_2': 3.894,
     'hgrn_lower_bounds_2': 33.114,
     'hgrn_out_norm_2': 27.297,
     'ffn2_norm_2': 5.774,
     'final_norm_2': 8.327}
    for name, (base, spread) in spreads.items():
        noise = np.random.default_rng([zlib.crc32(name.encode()), seed]).standard_normal(out[name].shape)
        drawn = base * np.exp(spread * noise) if base else spread * noise
        out[name] = jnp.asarray(drawn.astype(out[name].dtype))
    for name, factor in factors.items():
        out[name] = (out[name] * factor).astype(out[name].dtype)
    return out
```

```python
import numpy as np

import concourse.bass as bass
from concourse import mybir
from contextlib import ExitStack

F32 = mybir.dt.float32
F32R = mybir.dt.float32r
BF16 = mybir.dt.bfloat16
I32 = mybir.dt.int32
U8 = mybir.dt.uint8
ALU = mybir.AluOpType
ACT = mybir.ActivationFunctionType
AX = mybir.AxisListType

P = 128
T = 256
D = 1024
KC = D // P
FF = 2816
GROUPS = FF // 256
LAYERS = 2
UNIT = 2048
RAW = 2
EPS = 1e-6
NEG = -1e30
EXP_LN_SET = 6

MIX1 = ["gr0", "gr1", "gq", "gk", "gv0", "gv1", "nq0", "nk0", "nv0", "nq1", "nk1", "nv1"]
MIX2 = ["hf0", "hf1", "hq0", "hq1", "hi0", "hi1", "hg0", "hg1", "fq", "fk", "fv", "dq", "dk", "dv"]
MIX = [MIX1, MIX2]
TOKEN_MAJOR = {"gv0", "gv1", "nv0", "nv1", "hi0", "hi1", "fv", "dv"}
STEPS = ["diag", 32, 16, 8, 4, 2, 1, 64, 128]
MASKED = [32, 16, 8, 4, 2, 1, 64]
UNITS_OUT = 4
SLOT_USES = [[2 * GROUPS + len([i for i in range(len(m) + UNITS_OUT) if i % 3 == s]) for s in range(3)]
             for m in MIX]
PCOLS = {"ffn1": (0, 8), "mix": (8, 8), "ffn2": (16, 8), "ogain": (24, 4), "rgain": (28, 4), "bias": (32, 4)}
PN = 36


def col_source(b, name):
    if b == 0:
        base = {"nq": 0, "nk": 512, "nv": 1024, "gq": 1536, "gk": 1792, "gv": 2048, "gr": 2560}
    else:
        base = {"fq": 0, "fk": 256, "fv": 512, "dq": 772, "dk": 1028, "dv": 1284,
                "hq": 1540, "hf": 2052, "hi": 2564, "hg": 3076}
    return base[name[:2]] + (256 * int(name[2]) if len(name) > 2 else 0)


CODE_COL, FORGET_COL = 3072, 768
OUT_PAIRS = [2, 3, 0, 1]


def build(nc, stream0, stream1, stream2, xt, params, final_gain, code_w, gate_w, forget_w, rpb,
          lower, positions, forget_bias, c_square, c_level, c_col, c_att, c_freq, c_sel, c_reset, out):
    ctx = ExitStack()
    with ctx:
        def sb(name, shape, dt=F32):
            return ctx.enter_context(nc.sbuf_tensor(name, shape, dt))

        def sem(name):
            return ctx.enter_context(nc.semaphore(name))

        streams = [stream0, stream1, stream2]
        raw = [sb(f"raw{s}", [P, RAW, UNIT]) for s in range(3)]
        w_hi = [sb(f"w_hi{s}", [P, UNIT], F32R) for s in range(3)]
        w_lo = [sb(f"w_lo{s}", [P, UNIT], F32R) for s in range(3)]
        x = sb("x", [P, KC, T])
        h = sb("h", [P, KC, T])
        h_hi = sb("h_hi", [P, KC, T], F32R)
        h_lo = sb("h_lo", [P, KC, T], F32R)
        scratch = sb("scratch", [P, 2, 512])
        act_hi = sb("act_hi", [P, 2, T], F32R)
        act_lo = sb("act_lo", [P, 2, T], F32R)
        rs = sb("rs", [P, T])
        square = sb("square", [P, 2, P])
        ident, ones = square[:, 0, :], square[:, 1, :]
        rot_m = sb("rot_m", [P, P])
        zero = sb("zero", [P, P], BF16)
        level = sb("level", [P, 2, len(MASKED), P], U8)
        reset = sb("reset", [P, T])
        cos_sin = sb("cos_sin", [P, 2, T])
        par_all = sb("par_all", [P, 2 * LAYERS, PN])
        par = sb("par", [P, PN])
        fgain = sb("fgain", [P, 2, KC])
        freq = sb("freq", [P, 1])
        eps = sb("eps", [P, 1])
        lb = sb("lb", [P, LAYERS, 4])
        lbt = sb("lbt", [P, 4, 4])
        lb_all = sb("lb_all", [P, LAYERS, 3, 4])
        lbs = sb("lbs", [P, 3, 4])
        col_mask = sb("col_mask", [P, 64])
        stat = sb("stat", [P, 2, 6])
        tot = sb("tot", [P, 4, 5])
        fbias = sb("fbias", [4, 1])

        ARENA = 15872
        arena = sb("arena", [P, ARENA])

        def part(at, *shape):
            n = 1
            for k in shape:
                n *= k
            names = "abcd"[:len(shape)]
            view = arena[:, at:at + n]
            if len(shape) == 1:
                return view
            return view.rearrange(f"p ({' '.join(names)}) -> p {' '.join(names)}",
                                  **{names[i]: shape[i] for i in range(1, len(shape))})

        aq, ak = part(0, 4, T), part(1024, 4, T)
        av = part(2048, 2, 512)
        rv = part(3072, 2, 512)
        rg = part(4096, 4, T)
        cum = part(5120, 4, T)
        dec = part(6144, 4, T)
        decay_A = part(7168, 2, 4, T)
        pT = part(9216, 2, 512)
        codes, cw = part(9216, T), part(9216 + T, KC, 32)
        qk1, qks1 = part(10240, 2, 2, T), part(11264, 2, 2, T)
        qk2, qks2 = part(10240, 2, 4, T), part(12288, 2, 4, T)
        gw = part(12288, 512)
        bias_t = part(12800, 8, 6, 64)
        att_mask = part(14336, 2, 2, T)
        fw = part(9216 + T, KC, 4)
        sel = part(15360, 4, P)[0:4]
        fc = part(5120, 3, T)[0:4]

        bank = [ctx.enter_context(nc.psum_tensor(f"bank{i}", [P, 512], F32)) for i in range(8)]
        PB, PD, PX = bank[0:2], bank[2:6], bank[6:8]
        SC = [PX, PD[2:4]]

        consts_loaded, x_loaded, small_loaded, bias_loaded = sem("consts_loaded"), sem("x_loaded"), sem("small_loaded"), sem("bias_loaded")
        mask2_loaded = sem("mask2_loaded")
        raw_ready = [sem(f"raw_ready{s}") for s in range(3)]
        hi_done = [sem(f"hi_done{s}") for s in range(3)]
        lo_done = [sem(f"lo_done{s}") for s in range(3)]
        used = [sem(f"used{s}") for s in range(3)]
        eg_ready = sem("eg_ready")
        a_ready, ahi_ready, alo_ready = sem("a_ready"), sem("ahi_ready"), sem("alo_ready")
        x_ready, sq_ready, ms_ready = sem("x_ready"), sem("sq_ready"), sem("ms_ready")
        rs_ready, h_ready, hhi_ready, hlo_ready = sem("rs_ready"), sem("h_ready"), sem("hhi_ready"), sem("hlo_ready")
        evicted = sem("evicted")
        code_ready, code_copied, z_ready, z_copied = sem("code_ready"), sem("code_copied"), sem("z_ready"), sem("z_copied")
        logit_ready, softplus_ready = sem("logit_ready"), sem("softplus_ready")
        d_ready, e_ready, qks_ready, span_ready, span_copied = sem("d_ready"), sem("e_ready"), sem("qks_ready"), sem("span_ready"), sem("span_copied")
        o_ready, o_sq, o_ms, o_rs = sem("o_ready"), sem("o_sq"), sem("o_ms"), sem("o_rs")
        mix_ready, mixhi_ready, mixlo_ready = sem("mix_ready"), sem("mixhi_ready"), sem("mixlo_ready")
        score_ready, max_ready, exp_ready, p_ready = sem("score_ready"), sem("max_ready"), sem("exp_ready"), sem("p_ready")
        pt_ready, pt_copied, head_ready, head_copied = sem("pt_ready"), sem("pt_copied"), sem("head_ready"), sem("head_copied")
        nsq, nms, nrs = sem("nsq"), sem("nms"), sem("nrs")
        rot_ready, rot_done, lb_step, ang_ready, trig_ready = sem("rot_ready"), sem("rot_done"), sem("lb_step"), sem("ang_ready"), sem("trig_ready")
        const_set, stored, bias_masked = sem("const_set"), sem("stored"), sem("bias_masked")
        layer_par = sem("layer_par")
        gsilu, rg_done = sem("gsilu"), sem("rg_done")
        heads_done = sem("heads_done")
        span_seen, load_issued = sem("span_seen"), sem("load_issued")

        def use(b, L, s, off):
            return b * LAYERS * SLOT_USES[0][s] + L * SLOT_USES[b][s] + off

        def mix_use(b, L, i):
            return i % 3, use(b, L, i % 3, GROUPS + i // 3)

        def ffn_use(b, L, j, s, g):
            return use(b, L, s, g + (SLOT_USES[b][s] - GROUPS if j else 0))

        def norm_no(b, L, j):
            return 7 * b + 3 * L + j

        def split_no(b, L, j):
            return 6 * b + 3 * L + j

        def unit_no(b, L, i):
            return b * LAYERS * len(MIX1) + L * len(MIX[b]) + i

        def ffn_no(b, L, j, g):
            return (4 * b + 2 * L + j) * GROUPS + g

        def layer_no(b, L):
            return 2 * b + L

        FIRST_STEP = [3, 5]

        block = ctx.enter_context(nc.Block())

        @block.sync
        def _(sp):
            def load(s, n):
                place, unit = sp.snap(n % RAW), sp.snap(n)
                sp.wait_ge(lo_done[s], n + 1)
                sp.sem_inc(load_issued, 1)
                sp.wait_ge(raw_ready[s], 16 * n + 16)
                sp.sem_inc(load_issued, 1)
                sp.dma_start(raw[s][:, bass.ds(place, 1), :], streams[s][bass.ds(unit, 1), :, :].rearrange("a p n -> p a n"))\
                    .then_inc(raw_ready[s], 16)

            with sp.Fori(0, LAYERS) as L:
                first = GROUPS + (len(MIX1) + UNITS_OUT) // 3
                with sp.Fori(0, first) as i:
                    for s in range(3):
                        load(s, use(0, L, s, i))
                load(0, use(0, L, 0, first))
                with sp.Fori(0, GROUPS) as i:
                    for s in range(3):
                        load(s, ffn_use(0, L, 1, s, i))
            with sp.Fori(0, LAYERS * SLOT_USES[1][0]) as i:
                for s in range(3):
                    load(s, use(1, 0, s, i))
            sp.wait_ge(x_ready, 4 * 14 + 4)
            sp.dma_start(out, x[:, :, :]).then_inc(stored, 16)
            sp.wait_ge(stored, 16)

        @block.gpsimd
        def _(pool):
            n = [0]

            def const(dst, src):
                pool.dma_start(dst, src).then_inc(consts_loaded, 16)
                n[0] += 1

            pool.dma_start(x[:, :, :], xt).then_inc(x_loaded, 16)
            const(square[:, :, :], c_square[:, 0:2, :])
            const(rot_m[:, :], c_square[:, 2, :])
            const(part(0, 2 * len(MASKED) * P).bitcast(I32), c_level.rearrange("p a b c -> p (a b c)"))
            const(reset[:, :], c_reset)
            const(par_all[:, :, :], params)
            const(fgain[:, :, :], final_gain)
            const(freq[:, :], c_freq)
            const(lb[:, :, :], lower)
            const(col_mask[:, :], c_col)
            const(scratch[:, 0, 0:T].bitcast(I32), bass.AP(tensor=positions.tensor, offset=0, ap=[[0, P], [1, T]]))
            assert n[0] == N_CONSTS
            pool.memset(zero[:, :], 0.0).then_inc(const_set, 1)
            pool.memset(eps[:, :], EPS).then_inc(const_set, 1)
            with pool.Fori(0, LAYERS) as L:
                pool.wait_ge(heads_done, L + 1)
                pool.dma_start(cw[:, :, :], code_w[bass.ds(L, 1), :, :, :].rearrange("a p k c -> p (a k) c"))\
                    .then_inc(small_loaded, 16)
                pool.dma_start(gw[0:32, :], gate_w[bass.ds(L, 1), :, :].rearrange("a p c -> p (a c)"))\
                    .then_inc(small_loaded, 16)
                for qr in range(2):
                    for hd in range(8):
                        row = rpb[bass.ds((L * 8 + hd) * 465 + (5 - qr) * 31 - 48, 1)]
                        src = bass.AP(tensor=row.tensor, offset=row.offset, ap=[[1, 64], [31, 6], [1, 64]])
                        pool.dma_start(bias_t[64 * qr:64 * qr + 64, hd, :, :], src).then_inc(bias_loaded, 16)
                pool.wait_ge(bias_loaded, 256 * L + 256)
                flat = bias_t.rearrange("p a b c -> p (a b) c")
                pool.tensor_tensor(flat, flat, col_mask[:, None, :].to_broadcast((P, 48, 64)), ALU.add)\
                    .then_inc(bias_masked, 1)
            pool.wait_ge(heads_done, LAYERS + 1)
            pool.dma_start(att_mask[:, :, :, :], c_att).then_inc(mask2_loaded, 16)
            pool.dma_start(sel[:, :, :], c_sel).then_inc(mask2_loaded, 16)
            with pool.Fori(0, LAYERS) as L:
                pool.wait_ge(heads_done, L + LAYERS + 1)
                pool.dma_start(fw[:, :, :], forget_w[bass.ds(L, 1), :, :, :].rearrange("a p k c -> p (a k) c"))\
                    .then_inc(small_loaded, 16)
                pool.dma_start(fbias[:, :], forget_bias[bass.ds(L, 1), :, :].rearrange("a p c -> p (a c)"))\
                    .then_inc(small_loaded, 16)

        @block.tensor
        def _(pe):
            mm = nc.tensor.matmul

            def ready(s, n):
                pe.wait_ge(lo_done[s], n + RAW + 1)

            def column_unit(dst, s, token_major, first_norm=None):
                hi, lo = w_hi[s], w_lo[s]
                for c in range(2):
                    for k in range(KC):
                        if first_norm is not None and c == 0 and k % 2 == 0:
                            pe.wait_ge(hlo_ready, 4 * first_norm + k // 2 + 1)
                        o = dst[:, c * T:(c + 1) * T]
                        if token_major:
                            tok = slice(c * P, (c + 1) * P)
                            w = slice(k * 256, (k + 1) * 256)
                            trio = [(h_hi[:, k, tok], hi[:, w]), (h_hi[:, k, tok], lo[:, w]), (h_lo[:, k, tok], hi[:, w])]
                        else:
                            w = slice(k * 256 + c * P, k * 256 + (c + 1) * P)
                            trio = [(hi[:, w], h_hi[:, k, :]), (hi[:, w], h_lo[:, k, :]), (lo[:, w], h_hi[:, k, :])]
                        for j, (a, r) in enumerate(trio):
                            last = mm(o, a, r, start=(k == 0 and j == 0), stop=(k == KC - 1 and j == 2))
                return last

            def row_unit(s, chunks_hi, chunks_lo, final=False):
                for k in range(2):
                    for c in range(KC):
                        w = slice(k * D + c * P, k * D + (c + 1) * P)
                        o = PD[c // 2][:, (c % 2) * T:(c % 2 + 1) * T]
                        for j, (a, r) in enumerate(((w_hi[s], chunks_hi[:, k, :]), (w_hi[s], chunks_lo[:, k, :]), (w_lo[s], chunks_hi[:, k, :]))):
                            last = mm(o, a[:, w], r, start=False, stop=final and k == 1 and j == 2 and c % 2 == 1)
                return last

            def clear_accumulators():
                for d in PD:
                    mm(d[:, :], zero[:, :], square[:, :, :].rearrange("p a b -> p (a b)").bitcast(BF16), start=True, stop=False)

            def mean_square(nn):
                for k in range(KC):
                    if k % 2 == 0:
                        pe.wait_ge(sq_ready, 4 * nn + k // 2 + 1)
                    last = mm(PX[0][:, 0:T], ones, h[:, k, :], start=(k == 0), stop=(k == KC - 1))
                last.then_inc(ms_ready, 1)

            def ffn(b, L, j):
                nn = norm_no(b, L, 2 * j)
                mean_square(nn)
                clear_accumulators()
                n = ffn_use(b, L, j, 0, 0)
                ready(0, n)
                column_unit(PB[0], 0, False, split_no(b, L, 2 * j)).then_inc(used[0], 1)
                ready(1, ffn_use(b, L, j, 1, 0))
                column_unit(PB[1], 1, False).then_inc(used[1], 1)

                def down(g, final=False):
                    pe.wait_ge(alo_ready, ffn_no(b, L, j, g) + 1)
                    ready(2, ffn_use(b, L, j, 2, g))
                    row_unit(2, act_hi, act_lo, final).then_inc(used[2], 1)

                with pe.Fori(1, GROUPS) as g:
                    pe.wait_ge(a_ready, ffn_no(b, L, j, g) + 1)
                    ready(0, ffn_use(b, L, j, 0, g))
                    column_unit(PB[0], 0, False).then_inc(used[0], 1)
                    ready(1, ffn_use(b, L, j, 1, g))
                    column_unit(PB[1], 1, False).then_inc(used[1], 1)
                    down(g - 1)
                down(GROUPS - 1, final=True)

            def span_step(b, L, t):
                kind = STEPS[t]
                base = len(STEPS) * layer_no(b, L) + t
                pe.wait_ge(qks_ready, base + 1)
                if t >= 2:
                    pe.wait_ge(span_copied, base - 1)
                src = (qk1, qk2)[b] if kind == "diag" else (qks1, qks2)[b]
                for j in range(2):
                    if b == 1 and kind == 128 and j == 1:
                        continue
                    for hd in range(4):
                        if b == 0:
                            rows, ch = slice(64 * (hd % 2), 64 * (hd % 2) + 64), hd // 2
                        else:
                            rows, ch = slice(0, P), hd
                        tt = 1 - j if kind == 128 else j
                        o, at = (2 * (t % 2) + hd % 2, 2 * j + hd // 2) if b == 0 else (2 * (t % 2) + j, hd)
                        last = mm(PD[o][:, at * P:(at + 1) * P], src[rows, 1, ch, j * P:(j + 1) * P],
                                  src[rows, 0, ch, tt * P:(tt + 1) * P], start=True, stop=True)
                last.then_inc(span_ready, 1)

            def recurrence_out(b, L):
                pe.wait_ge(span_copied, len(STEPS) * (layer_no(b, L) + 1))
                for hd in range(4):
                    o = PD[hd // 2]
                    at = (hd % 2) * T
                    v0, v1 = rv[:, 0, hd * P:(hd + 1) * P], rv[:, 1, hd * P:(hd + 1) * P]
                    if b == 0:
                        mm(o[:, at:at + T], v0, decay_A[:, 0, hd, :], start=True, stop=False)
                        last = mm(o[:, at:at + T], v1, decay_A[:, 1, hd, :], start=False, stop=True)
                    else:
                        mm(o[:, at:at + P], v0, decay_A[:, 0, hd, 0:P], start=True, stop=True)
                        mm(o[:, at + P:at + T], v0, decay_A[:, 0, hd, P:T], start=True, stop=False)
                        last = mm(o[:, at + P:at + T], v1, decay_A[:, 1, hd, P:T], start=False, stop=True)
                last.then_inc(o_ready, 1)
                pe.wait_ge(o_sq, layer_no(b, L) + 1)
                for i in range(2):
                    last = mm(PD[2 + i][:, :], ones, dec[:, 2 * i:2 * i + 2, :], start=True, stop=True)
                last.then_inc(o_ms, 1)

            def scores(b, L, i):
                hp, tile = i // 2, i % 2
                no = 8 * layer_no(b, L) + i
                if i >= 2:
                    pe.wait_ge(max_ready, no - 1)
                q = slice(tile * P, (tile + 1) * P)
                for e in range(2):
                    rows = slice(64 * e, 64 * e + 64)
                    fox = b == 1 and hp < 2
                    o = SC[i % 2][e]
                    last = mm(o[:, 0:T], aq[rows, hp, q], ak[rows, hp, :], start=True, stop=not fox)
                    if fox:
                        hd = 2 * hp + e
                        mm(o[:, 0:T], sel[:, hd, :], fc[:, 1, :], start=False, stop=False)
                        last = mm(o[:, 0:T], fc[:, 0, q], sel[:, hd:hd + 1, :].to_broadcast((4, 2, P)), start=False, stop=True)
                last.then_inc(score_ready, 1)

            def transposes(b, L, i):
                no = 8 * layer_no(b, L) + i
                pe.wait_ge(p_ready, no + 1)
                if i >= 1:
                    pe.wait_ge(pt_copied, no)
                for n in range(4):
                    last = nc.tensor.transpose(PB[0][:, n * P:(n + 1) * P], scratch[:, i % 2, n * P:(n + 1) * P], ident)
                last.then_inc(pt_ready, 1)

            def heads(b, L, i):
                hp, tile = i // 2, i % 2
                no = 8 * layer_no(b, L) + i
                pe.wait_ge(pt_copied, no + 1)
                if i >= 1:
                    pe.wait_ge(head_copied, no)
                for e in range(2):
                    for kt in range(2):
                        last = mm(PB[1][64 * e:64 * e + 64, 0:P], av[:, kt, hp * P + 64 * e:hp * P + 64 * e + 64],
                                  pT[:, i % 2, (2 * e + kt) * P:(2 * e + kt + 1) * P], start=(kt == 0), stop=(kt == 1))
                last.then_inc(head_ready, 1)

            def mixing(b, L):
                nn = norm_no(b, L, 1)
                mean_square(nn)
                width = (32, 4)[b]
                w = (cw, fw)[b]
                pe.wait_ge(small_loaded, 32 * (layer_no(b, L) + 1))
                pe.wait_ge(h_ready, 4 * split_no(b, L, 1) + 4)
                for k in range(KC):
                    last = mm(PX[1][0:width, 0:T], w[:, k, :], h[:, k, :], start=(k == 0), stop=(k == KC - 1))
                last.then_inc(code_ready, 1)
                for i, name in enumerate(MIX[b]):
                    s, n = mix_use(b, L, i)
                    ready(s, n)
                    if i >= 2:
                        pe.wait_ge(evicted, unit_no(b, L, i) - 1)
                    column_unit(PB[i % 2], s, name in TOKEN_MAJOR, split_no(b, L, 1) if i == 0 else None).then_inc(used[s], 1)
                    if b == 0 and i == 0:
                        pe.wait_ge(code_copied, L + 1)
                        for c in range(4):
                            last = mm(PD[c // 2][:, (c % 2) * T:(c % 2 + 1) * T], gw[0:32, c * P:(c + 1) * P], codes[0:32, :],
                                      start=True, stop=True)
                        last.then_inc(z_ready, 1)
                    if i >= FIRST_STEP[b]:
                        span_step(b, L, i - FIRST_STEP[b])
                pe.wait_ge(evicted, unit_no(b, L, len(MIX[b])))
                recurrence_out(b, L)
                if b == 1:
                    pe.wait_ge(mask2_loaded, 32)
                    for i in range(2):
                        if i:
                            pe.wait_ge(rot_done, 2 * L + 1)
                        mm(PX[0][:, :], rot_m[:, :], (aq, ak)[i][:, 2:4, :], start=True, stop=True).then_inc(rot_ready, 1)
                    pe.wait_ge(rot_done, 2 * L + 2)
                scores(b, L, 0)
                pe.wait_ge(o_rs, layer_no(b, L) + 1)
                for i in range(8):
                    if i < 7:
                        scores(b, L, i + 1)
                    transposes(b, L, i)
                    heads(b, L, i)
                if b == 0:
                    pe.wait_ge(nsq, L + 1)
                    for c in range(4):
                        last = mm(PX[0][:, 0:T], ones, dec[:, c, :], start=(c == 0), stop=(c == 3))
                    last.then_inc(nms, 1)
                for i, pair in enumerate(OUT_PAIRS):
                    pe.wait_ge(mixlo_ready, 4 * layer_no(b, L) + i + 1)
                    if i == 0:
                        clear_accumulators()
                    s, n = mix_use(b, L, len(MIX[b]) + i)
                    ready(s, n)
                    row_unit(s, h_hi[:, 2 * pair:2 * pair + 2, :], h_lo[:, 2 * pair:2 * pair + 2, :], final=i == 3).then_inc(used[s], 1)

            for s in range(3):
                pe.sem_inc(used[s], 1)
            pe.wait_ge(const_set, 2)
            pe.wait_ge(consts_loaded, 16 * N_CONSTS)
            for b in range(2):
                with pe.Fori(0, LAYERS) as L:
                    ffn(b, L, 0)
                    mixing(b, L)
                    ffn(b, L, 1)
                mean_square(norm_no(b, LAYERS, 0))

        @block.scalar
        def _(act):
            fn = nc.scalar.activation

            def split(s, n):
                act.wait_ge(raw_ready[s], 16 * n + 32)
                act.wait_ge(used[s], n + 1)
                fn(w_hi[s][:, :], raw[s][:, bass.ds(n % RAW, 1), :].rearrange("p a n -> p (a n)"), ACT.Copy).then_inc(hi_done[s], 1)

            def norm(nn, sn=None):
                for k in range(4):
                    act.wait_ge(x_ready, 4 * nn + k + 1)
                    fn(h[:, 2 * k:2 * k + 2, :], x[:, 2 * k:2 * k + 2, :], ACT.Square).then_inc(sq_ready, 1)
                act.wait_ge(ms_ready, nn + 1)
                rsqrt(rs[:, :], PX[0][:, 0:T], 1.0 / D).then_inc(rs_ready, 1)
                if sn is not None:
                    for k in range(4):
                        act.wait_ge(h_ready, 4 * sn + k + 1)
                        fn(h_hi[:, 2 * k:2 * k + 2, :], h[:, 2 * k:2 * k + 2, :], ACT.Copy).then_inc(hhi_ready, 1)

            def rsqrt(dst, src, scale):
                fn(dst, src, ACT.Ln, bias=eps[:, :], scale=scale)
                act.drain()
                return fn(dst, dst, ACT.Exp, scale=-0.5)

            def ffn(b, L, j):
                nn = norm_no(b, L, 2 * j)
                for s in range(2):
                    split(s, ffn_use(b, L, j, s, 0))
                norm(nn, split_no(b, L, 2 * j))

                def gate_exp(g):
                    act.wait_ge(used[0], ffn_use(b, L, j, 0, g) + 2)
                    act.wait_ge(a_ready, ffn_no(b, L, j, g) + 1)
                    fn(scratch[:, 0, :], PB[0][:, :], ACT.Exp, scale=-1.0).then_inc(eg_ready, 1)

                def gated_hi(g):
                    act.wait_ge(a_ready, ffn_no(b, L, j, g) + 2)
                    act.wait_ge(used[2], ffn_use(b, L, j, 2, g) + 1)
                    fn(act_hi[:, :, :].rearrange("p a b -> p (a b)"), scratch[:, 1, :], ACT.Copy).then_inc(ahi_ready, 1)

                with act.Fori(1, GROUPS) as g:
                    split(0, ffn_use(b, L, j, 0, g))
                    gate_exp(g - 1)
                    split(1, ffn_use(b, L, j, 1, g))
                    gated_hi(g - 1)
                    split(2, ffn_use(b, L, j, 2, g - 1))
                gate_exp(GROUPS - 1)
                gated_hi(GROUPS - 1)
                split(2, ffn_use(b, L, j, 2, GROUPS - 1))

            def evict(b, L, i):
                name = MIX[b][i]
                slot, n = mix_use(b, L, i)
                act.wait_ge(used[slot], n + 2)
                src = PB[i % 2][:, :]
                kind, half = name[:2], int(name[2]) if len(name) > 2 else 0
                two = src.rearrange("p (c t) -> p c t", c=2)
                scale = 0.125 if kind in ("nq", "gq", "fq", "dq") else 1.0
                if kind == "nq":
                    for c in range(2):
                        dst = aq[:, 2 * half + c, :]
                        rev = bass.AP(tensor=dst.tensor, offset=dst.offset + 63, ap=[dst.ap[0], [64, 4], [-1, 64]])
                        ins = fn(rev, src[:, c * T:(c + 1) * T].rearrange("p (r c) -> p r c", c=64), ACT.Copy, scale=scale)
                elif kind == "hg":
                    ins = fn(rg[:, 2 * half:2 * half + 2, :], two, ACT.Exp, scale=-1.0)
                else:
                    if kind == "gr":
                        fn(qks1.rearrange("p a b t -> p (a b) t")[:, 2 * half:2 * half + 2, :], two, ACT.Exp, scale=-1.0)
                    if kind == "hq":
                        fn(decay_A[:, 0, 2 * half:2 * half + 2, :], two, ACT.Exp, scale=-1.0)
                    dst = {"nk": lambda: ak[:, 2 * half:2 * half + 2, :], "gr": lambda: rg[:, 2 * half:2 * half + 2, :],
                           "nv": lambda: av[:, :, 256 * half:256 * half + 256], "gv": lambda: rv[:, :, 256 * half:256 * half + 256],
                           "hi": lambda: rv[:, :, 256 * half:256 * half + 256],
                           "fv": lambda: av[:, :, 0:256], "dv": lambda: av[:, :, 256:512],
                           "fq": lambda: aq[:, 0:2, :], "fk": lambda: ak[:, 0:2, :],
                           "dq": lambda: aq[:, 2:4, :], "dk": lambda: ak[:, 2:4, :],
                           "gq": lambda: qk1[:, 0, :, :], "gk": lambda: qk1[:, 1, :, :],
                           "hq": lambda: qk2[:, 0, 2 * half:2 * half + 2, :], "hf": lambda: qk2[:, 1, 2 * half:2 * half + 2, :]}[kind]()
                    ins = fn(dst, two, ACT.Copy, scale=scale)
                ins.then_inc(evicted, 1)

            def softplus(t, z, no):
                act.wait_ge(logit_ready, no + 1)
                fn(t, z, ACT.Abs)
                act.drain()
                fn(t, t, ACT.Exp, scale=-1.0)
                act.drain()
                fn(t, t, ACT.Ln, bias=1.0).then_inc(softplus_ready, 1)

            def span_exp(b, L, t):
                act.wait_ge(d_ready, (len(STEPS) - 1) * layer_no(b, L) + t)
                fn(dec[:, :, :], dec[:, :, :], ACT.Exp, scale=(1 / 16, 1.0)[b]).then_inc(e_ready, 1)

            def recurrence_out(b, L):
                act.wait_ge(o_ready, layer_no(b, L) + 1)
                for i in range(2):
                    ins = fn(dec[:, 2 * i:2 * i + 2, :].rearrange("p a b -> p (a b)"), PD[i][:, :], ACT.Square)
                ins.then_inc(o_sq, 1)
                act.wait_ge(o_ms, layer_no(b, L) + 1)
                for i in range(2):
                    fn(cum[:, 2 * i:2 * i + 2, :].rearrange("p a b -> p (a b)"), PD[2 + i][:, :], ACT.Ln, bias=eps[:, :], scale=1.0 / P)
                act.drain()
                fn(cum[:, :, :], cum[:, :, :], ACT.Exp, scale=-0.5).then_inc(o_rs, 1)

            def mixing(b, L):
                lno = layer_no(b, L)
                nn = norm_no(b, L, 1)
                nunits = len(MIX[b])
                for i in range(3):
                    split(*mix_use(b, L, i))
                norm(nn, split_no(b, L, 1))
                if b == 0:
                    act.wait_ge(code_ready, lno + 1)
                    fn(codes[0:32, :], PX[1][0:32, 0:T], ACT.Copy).then_inc(code_copied, 1)
                for i in range(nunits):
                    evict(b, L, i)
                    split(*mix_use(b, L, i + 3))
                    if b == 0 and i == 1:
                        softplus(qks1.rearrange("p a b t -> p (a b) t"), dec[:, :, :], L)
                    if b == 1 and i == 1:
                        softplus(dec[:, :, :], qk2[:, 1, :, :], LAYERS + 2 * L)
                        act.wait_ge(gsilu, L + 1)
                        fn(qk2[:, 1, :, :], qk2[:, 1, :, :], ACT.Exp)
                        fn(qks2[:, 0, :, :], qks2[:, 0, :, :], ACT.Exp)
                        act.drain()
                        fn(qks2[:, 0, :, :], qks2[:, 0, :, :], ACT.Ln, bias=1.0).then_inc(rg_done, 1)
                    t = i - FIRST_STEP[b] + 1
                    if 1 <= t < len(STEPS):
                        span_exp(b, L, t)
                recurrence_out(b, L)
                if b == 1:
                    softplus(fc[:, 2, :], fc[:, 0, :], LAYERS + 2 * L + 1)

                def softmax(i):
                    no = 8 * lno + i
                    act.wait_ge(max_ready, no + 1)
                    for e in range(2):
                        fn(scratch[:, i % 2, e * T:(e + 1) * T], scratch[:, i % 2, e * T:(e + 1) * T], ACT.Exp,
                           bias=stat[:, i % 2, e:e + 1], accum_out=stat[:, i % 2, 2 + e:3 + e])
                    act.drain().then_inc(exp_ready, 1)

                def copy_pt(i):
                    no = 8 * lno + i
                    act.wait_ge(pt_ready, no + 1)
                    if i >= 2:
                        act.wait_ge(head_ready, no - 1)
                    fn(pT[:, i % 2, :], PB[0][:, :], ACT.Copy).then_inc(pt_copied, 1)

                def copy_head(i):
                    hp, tile = i // 2, i % 2
                    no = 8 * lno + i
                    act.wait_ge(head_ready, no + 1)
                    dst = h[:, hp, tile * P:(tile + 1) * P]
                    if b == 0:
                        rev = bass.AP(tensor=dst.tensor, offset=dst.offset + 63, ap=[dst.ap[0], [64, 2], [-1, 64]])
                        fn(rev, PB[1][:, 0:P].rearrange("p (r c) -> p r c", c=64), ACT.Copy).then_inc(head_copied, 1)
                    else:
                        fn(dst, PB[1][:, 0:P], ACT.Copy).then_inc(head_copied, 1)

                def split_mixed(k):
                    act.wait_ge(mix_ready, 4 * lno + k + 1)
                    pair = OUT_PAIRS[k]
                    fn(h_hi[:, 2 * pair:2 * pair + 2, :], h[:, 2 * pair:2 * pair + 2, :], ACT.Copy).then_inc(mixhi_ready, 1)

                for i in range(8):
                    softmax(i)
                    if i >= 1:
                        copy_pt(i - 1)
                        copy_head(i - 1)
                copy_pt(7)
                copy_head(7)
                for k in range(2):
                    split_mixed(k)
                if b == 0:
                    act.drain()
                    fn(dec[:, :, :], h[:, 0:4, :], ACT.Square).then_inc(nsq, 1)
                    act.wait_ge(nms, L + 1)
                    rsqrt(rs[:, :], PX[0][:, 0:T], 1.0 / 512).then_inc(nrs, 1)
                for k in range(2, 4):
                    split_mixed(k)
                split(*mix_use(b, L, nunits + 3))

            act.wait_ge(ang_ready, 1)
            fn(cos_sin[:, :, :], cos_sin[:, :, :], ACT.Sin).then_inc(trig_ready, 1)
            act.add_instruction(mybir.InstLoadActFuncSet(name=nc.get_next_instruction_name(), act_func_set_id=EXP_LN_SET, ins=[], outs=[]))
            act.wait_ge(lb_step, 1)
            fn(lbt[:, 0:2, :], lbt[:, 0:2, :], ACT.Exp).then_inc(lb_step, 1)
            act.wait_ge(lb_step, 3)
            fn(lb_all[:, :, 0, :], lb_all[:, :, 0, :], ACT.Ln, scale=2.0 ** 40)
            fn(lb_all[:, :, 1, :], lb_all[:, :, 2, :], ACT.Ln).then_inc(lb_step, 1)
            for b in range(2):
                with act.Fori(0, LAYERS) as L:
                    ffn(b, L, 0)
                    mixing(b, L)
                    ffn(b, L, 1)
                norm(norm_no(b, LAYERS, 0))

        @block.vector
        def _(dve):
            v = nc.vector
            tt, ts, stt = v.tensor_tensor, v.tensor_scalar, v.scalar_tensor_tensor

            def wide(ap, *shape):
                return ap.to_broadcast(shape)

            def split(s, n):
                dve.wait_ge(hi_done[s], n + 1)
                tt(w_lo[s][:, :], raw[s][:, bass.ds(n % RAW, 1), :].rearrange("p a n -> p (a n)"), w_hi[s][:, :].bitcast(F32),
                   ALU.subtract).then_inc(lo_done[s], 1)

            def gain(col, k):
                return par[:, PCOLS[col][0] + k:PCOLS[col][0] + k + 1]

            def norm(nn, sn, col):
                dve.wait_ge(rs_ready, nn + 1)
                for k in range(KC):
                    ins = stt(h[:, k, :], x[:, k, :], gain(col, k), rs[:, :], ALU.mult, ALU.mult)
                    if k % 2:
                        ins.then_inc(h_ready, 1)
                for k in range(4):
                    dve.wait_ge(hhi_ready, 4 * sn + k + 1)
                    two = slice(2 * k, 2 * k + 2)
                    tt(h_lo[:, two, :], h[:, two, :], h_hi[:, two, :].bitcast(F32), ALU.subtract).then_inc(hlo_ready, 1)

            def update(s, n, scale):
                dve.wait_ge(used[s], n + 2)
                for k in range(4):
                    two = x[:, 2 * k:2 * k + 2, :].rearrange("p a b -> p (a b)")
                    stt(two, PD[k][:, :], scale, two, ALU.mult, ALU.add).then_inc(x_ready, 1)

            def ffn(b, L, j):
                nn = norm_no(b, L, 2 * j)
                for s in range(2):
                    split(s, ffn_use(b, L, j, s, 0))
                norm(nn, split_no(b, L, 2 * j), ("ffn1", "ffn2")[j])

                def gated(g):
                    dve.wait_ge(eg_ready, ffn_no(b, L, j, g) + 1)
                    e = scratch[:, 0, :]
                    ts(e, e, 1.0, None, ALU.add)
                    dve.drain()
                    v.reciprocal(e, e)
                    dve.drain()
                    tt(e, e, PB[0][:, :], ALU.mult)
                    dve.drain()
                    dve.wait_ge(used[1], ffn_use(b, L, j, 1, g) + 2)
                    tt(scratch[:, 1, :], e, PB[1][:, :], ALU.mult).then_inc(a_ready, 1)

                def gated_lo(g):
                    dve.wait_ge(ahi_ready, ffn_no(b, L, j, g) + 1)
                    tt(act_lo[:, :, :].rearrange("p a b -> p (a b)"), scratch[:, 1, :],
                       act_hi[:, :, :].rearrange("p a b -> p (a b)").bitcast(F32), ALU.subtract).then_inc(alo_ready, 1)

                with dve.Fori(1, GROUPS) as g:
                    split(0, ffn_use(b, L, j, 0, g))
                    gated(g - 1)
                    split(1, ffn_use(b, L, j, 1, g))
                    gated_lo(g - 1)
                    split(2, ffn_use(b, L, j, 2, g - 1))
                gated(GROUPS - 1)
                gated_lo(GROUPS - 1)
                split(2, ffn_use(b, L, j, 2, GROUPS - 1))
                update(2, ffn_use(b, L, j, 2, GROUPS - 1), 0.5)

            def halves(ap, m):
                w = ap.rearrange("p c (n two m) -> p (c n) two m", two=2, m=m)
                return w[:, :, 0, :], w[:, :, 1, :]

            def less(dst, a, r):
                shape = tuple(dst.shape)
                a = a if tuple(a.shape) == shape else wide(a, *shape)
                r = r if tuple(r.shape) == shape else wide(r, *shape)
                return tt(dst, a, r, ALU.subtract)

            def chunk(ap, c):
                return ap[:, :, 64 * c:64 * c + 64]

            def span_decay(b, L, t):
                m = STEPS[t]
                fq, fk = (dec[:, 0:2, :], dec[:, 2:4, :]) if b == 0 else (dec[:, :, :], dec[:, :, :])
                fx, ft = (cum[:, 0:2, :], tot[:, 0:2, :]) if b == 0 else (cum[:, :, :], tot[:, :, :])
                bx, bt = cum[:, 2:4, :], tot[:, 2:4, :]
                if m <= 32:
                    (lo, up) = halves(fx, m)
                    ref = lo[:, :, m - 1:m]
                    less(halves(fq, m)[1], up, ref)
                    ins = less(halves(fk, m)[0], ref, lo)
                    if b == 0:
                        lo, up = halves(bx, m)
                        ref = up[:, :, 0:1]
                        less(halves(fq, m)[0], ref, lo)
                        ins = less(halves(fk, m)[1], up, ref)
                elif m == 64:
                    for a in range(2):
                        v.tensor_copy(chunk(fq, 2 * a + 1), chunk(fx, 2 * a + 1))
                        ins = less(chunk(fk, 2 * a), ft[:, :, 2 * a:2 * a + 1], chunk(fx, 2 * a))
                        if b == 0:
                            less(chunk(fq, 2 * a), bt[:, :, 2 * a:2 * a + 1], chunk(bx, 2 * a))
                            ins = v.tensor_copy(chunk(fk, 2 * a + 1), chunk(bx, 2 * a + 1))
                else:
                    def add(dst, a, r):
                        return tt(dst, a, wide(r, *dst.shape), ALU.add)
                    v.tensor_copy(chunk(fq, 2), chunk(fx, 2))
                    add(chunk(fq, 3), chunk(fx, 3), ft[:, :, 2:3])
                    less(chunk(fk, 1), ft[:, :, 1:2], chunk(fx, 1))
                    ins = less(chunk(fk, 0), ft[:, :, 4:5], chunk(fx, 0))
                    if b == 0:
                        less(chunk(fq, 1), bt[:, :, 1:2], chunk(bx, 1))
                        less(chunk(fq, 0), bt[:, :, 4:5], chunk(bx, 0))
                        v.tensor_copy(chunk(fk, 2), chunk(bx, 2))
                        ins = add(chunk(fk, 3), chunk(bx, 3), bt[:, :, 2:3])
                ins.then_inc(d_ready, 1)

            def span_scale(b, L, t):
                no = len(STEPS) * layer_no(b, L) + t
                if t == 0:
                    dve.sem_inc(qks_ready, 1)
                    return
                dve.wait_ge(e_ready, (len(STEPS) - 1) * layer_no(b, L) + t)
                dve.wait_ge(span_ready, no)
                if b == 0:
                    tt(qks1.rearrange("p a b t -> p (a b t)"), qk1.rearrange("p a b t -> p (a b t)"),
                       dec[:, :, :].rearrange("p a t -> p (a t)"), ALU.mult).then_inc(qks_ready, 1)
                else:
                    m = STEPS[t]
                    tt(halves(qks2[:, 0, :, :], m)[1], halves(qk2[:, 0, :, :], m)[1], halves(dec[:, :, :], m)[1], ALU.mult)
                    tt(halves(qks2[:, 1, :, :], m)[0], halves(qk2[:, 1, :, :], m)[0], halves(dec[:, :, :], m)[0], ALU.mult)\
                        .then_inc(qks_ready, 1)

            def span_copy(b, L, t):
                kind = STEPS[t]
                no = len(STEPS) * layer_no(b, L) + t
                dve.wait_ge(span_ready, no + 1)
                dve.sem_inc(span_seen, 1)
                for n in range(2):
                    if b == 1 and kind == 128 and n == 1:
                        continue
                    if b == 0:
                        swap = kind == 128
                        base = decay_A[:, 0, n, P if swap else 0:T]
                        dst = bass.AP(tensor=base.tensor, offset=base.offset,
                                      ap=[base.ap[0], [4 * T - P if swap else 4 * T + P, 2], [2 * T, 2], [1, P]])
                        src = PD[2 * (t % 2) + n][:, :].rearrange("p (j h t) -> p j h t", j=2, h=2)
                        spread = lambda m: wide(m[:, None, None, :], P, 2, 2, P)
                    else:
                        tile = 1 - n if kind == 128 else n
                        dst = decay_A[:, n, :, tile * P:(tile + 1) * P]
                        src = PD[2 * (t % 2) + n][:, :].rearrange("p (h t) -> p h t", h=4)
                        spread = lambda m: wide(m[:, None, :], P, 4, P)
                    if kind == "diag":
                        ins = tt(dst, src, spread(ident), ALU.mult)
                    elif kind == 128:
                        ins = v.tensor_copy(dst, src)
                    else:
                        ins = v.copy_predicated(dst, spread(level[:, b, MASKED.index(kind), :]), src)
                ins.then_inc(span_copied, 1)
                dve.drain()

            def scans(rows, src, dst):
                for c in range(4):
                    v.tensor_tensor_scan(dst[:, c, :], reset[:, :], src[:, c, :], 0.0, ALU.mult, ALU.add)
                dve.drain()
                v.tensor_copy(tot[:, :, 0:4], dst.rearrange("p c (n t) -> p c n t", t=64)[:, :, :, 63])
                dve.drain()
                tt(tot[:, :, 4:5], tot[:, :, 0:1], tot[:, :, 1:2], ALU.add)

            def gates(b, L):
                tmp = qks1.rearrange("p a b t -> p (a b) t")
                dve.wait_ge(z_ready, L + 1)
                for c in range(4):
                    ts(dec[:, c, :], PD[c // 2][:, (c % 2) * T:(c % 2 + 1) * T], gain("bias", c), None, ALU.add)
                dve.drain().then_inc(logit_ready, 1)
                dve.wait_ge(softplus_ready, L + 1)
                stt(dec[:, :, :], dec[:, :, :], 0.0, tmp, ALU.min, ALU.subtract)
                dve.drain()
                scans(4, dec, cum)
                tt(cum[:, 2:4, :], cum[:, 2:4, :], dec[:, 2:4, :], ALU.subtract)
                dve.drain()

            def forget_sums(L):
                z, t = fc[:, 0, :], fc[:, 2, :]
                dve.wait_ge(code_ready, LAYERS + L + 1)
                v.memset(fc[:, 1, :], 1.0)
                ts(z, PX[1][0:4, 0:T], fbias[:, :], None, ALU.add).then_inc(logit_ready, 1)
                dve.wait_ge(softplus_ready, LAYERS + 2 * L + 2)
                stt(z, z, 0.0, t, ALU.min, ALU.subtract)
                dve.drain()
                v.tensor_tensor_scan(t, fc[:, 1, :], z, 0.0, ALU.mult, ALU.add)
                dve.drain()
                ts(fc[:, 0, :], t, 1.0, None, ALU.mult)
                ts(fc[:, 1, :], t, -1.0, None, ALU.mult)

            def hgrn_gates(L):
                z, mx, mn = qk2[:, 1, :, :], qks2[:, 1, :, :], qks2[:, 0, :, :]
                dve.wait_ge(evicted, unit_no(1, L, 1) + 1)
                dve.sem_inc(logit_ready, 1)
                dve.wait_ge(softplus_ready, LAYERS + 2 * L + 1)
                stt(dec[:, :, :], z, 0.0, dec[:, :, :], ALU.min, ALU.subtract)
                dve.drain()
                tt(z, dec[:, :, :], z, ALU.subtract)
                tt(dec[:, :, :], dec[:, :, :], wide(lbs[:, 1, :, None], P, 4, T), ALU.add)
                dve.drain()
                tt(mx, dec[:, :, :], wide(lbs[:, 0, :, None], P, 4, T), ALU.max)
                tt(mn, dec[:, :, :], wide(lbs[:, 0, :, None], P, 4, T), ALU.min)
                dve.drain()
                tt(mn, mn, mx, ALU.subtract).then_inc(gsilu, 1)
                dve.wait_ge(rg_done, L + 1)
                tt(mx, mx, mn, ALU.add)
                tt(z, z, wide(lbs[:, 2, :, None], P, 4, T), ALU.mult)
                dve.drain()
                scans(4, mx, cum)
                dve.drain()

            def sigmoid_times(dst, e, times=True):
                ts(e, e, 1.0, None, ALU.add)
                dve.drain()
                v.reciprocal(e if times else dst, e)
                dve.drain()
                if times:
                    tt(dst, dst, e, ALU.mult)
                    dve.drain()

            def recurrence_out(b, L):
                lno = layer_no(b, L)
                dve.wait_ge(o_rs, lno + 1)
                for hd in range(4):
                    stt(h[:, 4 + hd, :], PD[hd // 2][:, (hd % 2) * T:(hd % 2 + 1) * T], gain("rgain", hd), cum[:, hd, :],
                        ALU.mult, ALU.mult)
                dve.drain()
                for k in range(2):
                    tt(h[:, 4 + 2 * k:6 + 2 * k, :], h[:, 4 + 2 * k:6 + 2 * k, :], rg[:, 2 * k:2 * k + 2, :], ALU.mult)\
                        .then_inc(mix_ready, 1)

            def mixed_lo(lno, k):
                dve.wait_ge(mixhi_ready, 4 * lno + k + 1)
                two = slice(2 * OUT_PAIRS[k], 2 * OUT_PAIRS[k] + 2)
                tt(h_lo[:, two, :], h[:, two, :], h_hi[:, two, :].bitcast(F32), ALU.subtract).then_inc(mixlo_ready, 1)

            def mixing(b, L):
                lno = layer_no(b, L)
                nunits = len(MIX[b])
                for i in range(3):
                    split(*mix_use(b, L, i))
                norm(norm_no(b, L, 1), split_no(b, L, 1), "mix")
                for i in range(nunits):
                    t = i - FIRST_STEP[b]
                    if t == 0:
                        dve.wait_ge(evicted, unit_no(b, L, 3) + 1)
                    if t >= 0:
                        span_scale(b, L, t)
                        if t + 1 < len(STEPS):
                            dve.drain()
                            span_decay(b, L, t + 1)
                    split(*mix_use(b, L, i + 3))
                    if b == 0 and i == 1:
                        dve.wait_ge(evicted, unit_no(b, L, 1) + 1)
                        sigmoid_times(rg[:, :, :], qks1.rearrange("p a b t -> p (a b) t"))
                        gates(b, L)
                    if b == 1 and i == 1:
                        hgrn_gates(L)
                    if b == 1 and i == 3:
                        dve.wait_ge(evicted, unit_no(b, L, 3) + 1)
                        sigmoid_times(qk2[:, 0, :, :], decay_A[:, 0, :, :])
                    if b == 1 and i == 8:
                        sigmoid_times(rg[:, :, :], rg[:, :, :], times=False)
                    if t >= 0:
                        span_copy(b, L, t)
                recurrence_out(b, L)
                if b == 1:
                    forget_sums(L)
                    dve.drain()
                    for i in range(2):
                        dve.wait_ge(rot_ready, 2 * L + i + 1)
                        y = (aq, ak)[i][:, 2:4, :]
                        tt(dec[:, 0:2, :], PX[0][:, :].rearrange("p (c t) -> p c t", c=2), wide(cos_sin[:, 1:2, :], P, 2, T), ALU.mult)
                        tt(y, y, wide(cos_sin[:, 0:1, :], P, 2, T), ALU.mult)
                        dve.drain()
                        tt(y, y, dec[:, 0:2, :], ALU.add).then_inc(rot_done, 1)
                        dve.drain()

                def masked(i):
                    hp, tile = i // 2, i % 2
                    no = 8 * lno + i
                    dve.wait_ge(score_ready, no + 1)
                    sc = scratch[:, i % 2, :].rearrange("p (e k) -> p e k", e=2)
                    if i >= 2:
                        dve.wait_ge(pt_ready, no - 1)
                    for e in range(2):
                        if b == 0:
                            extra = bias_t[:, 2 * hp + e, 2 - 2 * tile:6 - 2 * tile, :].rearrange("p r c -> p (r c)")
                        else:
                            extra = att_mask[:, hp // 2, tile, :]
                        tt(sc[:, e, :], SC[i % 2][e][:, 0:T], extra, ALU.add)
                    dve.drain()
                    v.tensor_reduce(stat[:, i % 2, 4:6], sc, AX.X, ALU.max)
                    dve.drain()
                    ts(stat[:, i % 2, 0:2], stat[:, i % 2, 4:6], -1.0, None, ALU.mult).then_inc(max_ready, 1)

                def normalise(i):
                    no = 8 * lno + i
                    dve.wait_ge(exp_ready, no + 1)
                    v.reciprocal(stat[:, i % 2, 2:4], stat[:, i % 2, 2:4])
                    dve.drain()
                    for e in range(2):
                        sc = scratch[:, i % 2, e * T:(e + 1) * T]
                        ins = ts(sc, sc, stat[:, i % 2, 2 + e:3 + e], None, ALU.mult)
                    ins.then_inc(p_ready, 1)

                if b == 0:
                    dve.wait_ge(bias_masked, L + 1)
                else:
                    dve.wait_ge(mask2_loaded, 32)
                masked(0)
                for i in range(8):
                    if i < 7:
                        masked(i + 1)
                    normalise(i)
                if b == 1:
                    dve.wait_ge(evicted, unit_no(b, L, nunits - 1) + 1)
                mixed_lo(lno, 0)
                mixed_lo(lno, 1)
                if b == 0:
                    dve.wait_ge(nrs, L + 1)
                    for k in range(2):
                        for c in range(2 * k, 2 * k + 2):
                            ins = stt(h[:, c, :], h[:, c, :], gain("ogain", c), rs[:, :], ALU.mult, ALU.mult)
                        ins.then_inc(mix_ready, 1)
                else:
                    dve.wait_ge(head_copied, 8 * lno + 8)
                    dve.sem_inc(mix_ready, 2)
                mixed_lo(lno, 2)
                mixed_lo(lno, 3)
                dve.drain().then_inc(heads_done, 1)
                split(*mix_use(b, L, nunits + 3))
                update(*mix_use(b, L, nunits + 3), 1.0)

            for s in range(3):
                dve.sem_inc(lo_done[s], RAW)
                dve.sem_inc(raw_ready[s], 16)
            dve.sem_inc(a_ready, 1)
            dve.sem_inc(heads_done, 1)
            dve.wait_ge(consts_loaded, 16 * N_CONSTS)
            v.tensor_copy(level[:, :, :, :].rearrange("p a b c -> p (a b c)"), part(0, 2 * len(MASKED) * P).bitcast(I32))
            posf, ang, turns = scratch[:, 0, T:2 * T], scratch[:, 1, 0:T], scratch[:, 1, T:2 * T]
            v.tensor_copy(posf, scratch[:, 0, 0:T].bitcast(I32))
            dve.drain()
            ts(ang, posf, freq[:, :], None, ALU.mult)
            dve.drain()
            ts(turns, ang, 1.0 / (2 * np.pi), None, ALU.mult)
            dve.drain()
            ts(turns, turns, ROUND, None, ALU.add)
            dve.drain()
            ts(turns, turns, ROUND, None, ALU.subtract)
            dve.drain()
            for piece in TWO_PI:
                stt(ang, turns, -piece, ang, ALU.mult, ALU.add)
                dve.drain()
            ts(posf, ang, float(np.pi / 2), None, ALU.is_gt)
            dve.drain()
            stt(posf, posf, float(-2 * np.pi), ang, ALU.mult, ALU.add)
            dve.drain()
            ts(posf, posf, float(np.pi / 2), None, ALU.add)
            dve.drain()
            for i, a in enumerate((posf, ang)):
                ins = ts(cos_sin[:, i, :], a, PI_IN, -PI_IN, ALU.min, ALU.max)
            ins.then_inc(ang_ready, 1)
            tt(lbt[:, 2, :], lb[:, 0, :], lb[:, 1, :], ALU.max)
            dve.drain()
            tt(lbt[:, 0:2, :], lb[:, :, :], wide(lbt[:, 2:3, :], P, 2, 4), ALU.subtract).then_inc(lb_step, 1)
            dve.wait_ge(lb_step, 2)
            tt(lbt[:, 2, :], lbt[:, 0, :], lbt[:, 1, :], ALU.add)
            dve.drain()
            v.reciprocal(lbt[:, 3, :], lbt[:, 2, :])
            dve.drain()
            tt(lbt[:, 0:2, :], lbt[:, 0:2, :], wide(lbt[:, 3:4, :], P, 2, 4), ALU.mult)
            dve.drain()
            tt(lbt[:, 2, :], lbt[:, 0, :], lbt[:, 1, :], ALU.add)
            dve.drain()
            tt(lb[:, 0, :], lbt[:, 0, :], lbt[:, 0, :], ALU.subtract)
            tt(lb[:, 1, :], lbt[:, 2, :], lbt[:, 0, :], ALU.subtract)
            dve.drain()
            ts(lb[:, :, :], lb[:, :, :], 0.0, 1.0 - 1e-6, ALU.max, ALU.min)
            dve.drain()
            ts(lb_all[:, :, 2, :], lb[:, :, :], -1.0, 1.0, ALU.mult, ALU.add)
            ts(lb_all[:, :, 0, :], lb[:, :, :], 1e-30, None, ALU.max).then_inc(lb_step, 1)
            dve.wait_ge(lb_step, 4)
            ts(lb_all[:, :, 0, :], lb_all[:, :, 0, :], float(40 * np.log(2.0)), None, ALU.subtract)
            dve.wait_ge(trig_ready, 1)
            dve.wait_ge(x_loaded, 16)
            dve.sem_inc(x_ready, 4)
            for b in range(2):
                with dve.Fori(0, LAYERS) as L:
                    v.tensor_copy(par[:, :], par_all[:, bass.ds(layer_no(b, L), 1), :].rearrange("p a n -> p (a n)"))
                    if b == 1:
                        v.tensor_copy(lbs[:, :, :].rearrange("p a b -> p (a b)"),
                                      lb_all[:, bass.ds(L, 1), :, :].rearrange("p a b c -> p (a b c)"))
                    dve.drain()
                    ffn(b, L, 0)
                    mixing(b, L)
                    ffn(b, L, 1)
                nn = norm_no(b, LAYERS, 0)
                dve.wait_ge(rs_ready, nn + 1)
                for k in range(KC):
                    ins = stt(x[:, k, :], x[:, k, :], fgain[:, b, k:k + 1], rs[:, :], ALU.mult, ALU.mult)
                    if k % 2:
                        ins.then_inc(x_ready, 1)
                dve.drain()


N_CONSTS = 10
ROUND = 1.5 * 2.0 ** 23
TWO_PI = [6.28125, 0.0019350051879882812, float(2 * np.pi - 6.28125 - 0.0019350051879882812)]
PI_IN = float(np.nextafter(np.float32(np.pi), np.float32(0)))


def constants():
    c = {}
    sq = np.zeros((P, 3, P), np.float32)
    sq[:, 0] = np.eye(P)
    sq[:, 1] = 1.0
    for i in range(P):
        j = i % 64
        if j < 8:
            sq[i + 8, 2, i] = -1.0
        elif j < 16:
            sq[i - 8, 2, i] = 1.0
    c["c_square"] = sq
    s, t = np.arange(P)[:, None], np.arange(P)[None, :]
    lv = np.zeros((P, 2, len(MASKED), P), np.int32)
    for i, m in enumerate(MASKED):
        same = s // (2 * m) == t // (2 * m)
        forward = same & (s // m % 2 == 0) & (t // m % 2 == 1)
        backward = same & (s // m % 2 == 1) & (t // m % 2 == 0)
        lv[:, 0, i] = forward | backward
        lv[:, 1, i] = forward
    c["c_level"] = lv
    qc = 63 - np.arange(P)[:, None] % 64
    kc = np.arange(64)[None, :]
    start = np.clip(qc - 8, 0, 48)
    c["c_col"] = np.where((kc >= start) & (kc < start + 16), 0.0, NEG).astype(np.float32)
    am = np.full((P, 2, 2, T), NEG, np.float32)
    for tile in range(2):
        q = tile * P + np.arange(P)[:, None]
        k = np.arange(T)[None, :]
        rel = q - k
        am[:, 0, tile] = np.where(rel >= 0, 0.0, NEG)
        times = (((rel >= 0) & (rel <= 128)).astype(int) + ((rel >= 0) & (rel % 4 == 0) & (rel <= 512))
                 + ((rel >= 0) & (rel % 16 == 0) & (rel <= 2048)))
        am[:, 1, tile] = np.where(times > 0, np.log(np.maximum(times, 1)), NEG)
    c["c_att"] = am
    f = 500000.0 ** (-np.arange(0, 16, 2, dtype=np.float32) / np.float32(16))
    j = np.arange(P) % 64
    c["c_freq"] = np.where(j < 16, f[j % 8], 0.0).astype(np.float32)[:, None]
    sel = np.zeros((4, 4, P), np.float32)
    for i in range(4):
        sel[i, i] = 1.0
    c["c_sel"] = sel
    c["c_reset"] = np.broadcast_to((np.arange(T) % 64 != 0).astype(np.float32), (P, T)).copy()
    return c


def column_layout(w, c, n=256):
    return w[:, c:c + n].reshape(KC, P, n).transpose(1, 0, 2)


def weight_streams(i):
    out = [[], [], []]
    names = [("ffn1_wg", "ffn1_wu", "ffn1_wd", "w_in", "w_out", "ffn2_wg", "ffn2_wu", "ffn2_wd"),
             ("ffn1_w_gate_2", "ffn1_w_up_2", "ffn1_w_down_2", "w_in_2", "w_out_2",
              "ffn2_w_gate_2", "ffn2_w_up_2", "ffn2_w_down_2")]
    for b in range(2):
        g1, u1, d1, w_in, w_out, g2, u2, d2 = (i[k] for k in names[b])
        for L in range(LAYERS):
            def ffn(g, u, d):
                for n in range(GROUPS):
                    out[0].append(column_layout(g[L], 256 * n).reshape(P, UNIT))
                    out[1].append(column_layout(u[L], 256 * n).reshape(P, UNIT))
                    out[2].append(d[L][256 * n:256 * n + 256].reshape(2, P, D).transpose(1, 0, 2).reshape(P, UNIT))
            ffn(g1, u1, d1)
            for n, name in enumerate(MIX[b]):
                out[n % 3].append(column_layout(w_in[L], col_source(b, name)).reshape(P, UNIT))
            for n, pair in enumerate(OUT_PAIRS):
                out[(len(MIX[b]) + n) % 3].append(w_out[L][256 * pair:256 * pair + 256].reshape(2, P, D).transpose(1, 0, 2).reshape(P, UNIT))
            ffn(g2, u2, d2)
    return [np.stack(o) for o in out]


def kernel(**inputs):
    import concourse.bacc as bacc
    from concourse.bass_utils import run_bass_kernel_spmd

    i = {k: np.asarray(v) for k, v in inputs.items()}

    def per_part(v):
        return v.reshape(-1, P).T

    arrays = {}
    for s, a in enumerate(weight_streams(i)):
        arrays[f"stream{s}"] = a
    arrays["xt"] = np.ascontiguousarray(i["x"][0].T.reshape(KC, P, T).transpose(1, 0, 2))
    pars = []
    for b, tail in enumerate(("", "_2")):
        for L in range(LAYERS):
            cols = [per_part(i[n + tail][L]) for n in ("ffn1_norm", "mix_norm", "ffn2_norm")]
            if b == 0:
                cols += [per_part(i["na_gain"][L])] + [per_part(i["gla_gain"][L])] * 4
                cols += [per_part(i["b_gate_f"][L]), per_part(i["b_gate_b"][L])]
            else:
                cols += [per_part(i["hgrn_out_norm_2"][L])] * 2 + [per_part(i["hgrn_out_norm_2"][L])]
            pars.append(np.concatenate(cols, 1))
    arrays["params"] = np.ascontiguousarray(np.stack(pars, 1))
    arrays["final_gain"] = np.ascontiguousarray(np.stack([per_part(i["final_norm"]), per_part(i["final_norm_2"])], 1))
    arrays["code_w"] = np.ascontiguousarray(np.stack([column_layout(i["w_in"][L], CODE_COL, 32) for L in range(LAYERS)]))
    gate_w = np.zeros((LAYERS, 32, 512), np.float32)
    gate_w[:, 0:16, 0:256] = i["w_gate_f"]
    gate_w[:, 16:32, 256:512] = i["w_gate_b"]
    arrays["gate_w"] = gate_w
    arrays["forget_w"] = np.ascontiguousarray(np.stack([column_layout(i["w_in_2"][L], FORGET_COL, 4) for L in range(LAYERS)]))
    arrays["rpb"] = np.ascontiguousarray(i["na_rpb"].reshape(-1))
    arrays["lower"] = np.ascontiguousarray(np.stack([per_part(i["hgrn_lower_bounds_2"][L]) for L in range(LAYERS)], 1))
    arrays["positions"] = np.ascontiguousarray(i["positions_2"].reshape(1, T))
    arrays["forget_bias"] = np.ascontiguousarray(i["fox_forget_bias_2"].reshape(LAYERS, 4, 1))
    arrays.update(constants())

    nc = bacc.Bacc("TRN2", target_bir_lowering=False, num_devices=1)
    args = [nc.dram_tensor(n, a.shape, mybir.dt.from_np(a.dtype), kind="ExternalInput").ap() for n, a in arrays.items()]
    out = nc.dram_tensor("out", (P, KC, T), F32, kind="ExternalOutput").ap()
    build(nc, *args, out)
    r = run_bass_kernel_spmd(nc, [arrays], core_ids=[0]).results[0]["out"]
    return np.ascontiguousarray(r.transpose(1, 0, 2).reshape(D, T).T)[None]
```

```python
import numpy as np

import concourse.bass as bass
from concourse import mybir
from contextlib import ExitStack

F32 = mybir.dt.float32
F32R = mybir.dt.float32r
BF16 = mybir.dt.bfloat16
I32 = mybir.dt.int32
U8 = mybir.dt.uint8
ALU = mybir.AluOpType
ACT = mybir.ActivationFunctionType
AX = mybir.AxisListType

P = 128
T = 256
D = 1024
KC = D // P
FF = 2816
GROUPS = FF // 256
LAYERS = 2
UNIT = 2048
RAW = 2
EPS = 1e-6
NEG = -1e30
EXP_LN_SET = 6

MIX1 = ["gq", "gk", "nq0", "nk0", "nv0", "gv0", "gv1", "nq1", "nk1", "nv1", "gr0", "gr1"]
MIX2 = ["hf0", "hf1", "hq0", "hq1", "fq", "fk", "fv", "dq", "dk", "dv", "hi0", "hi1", "hg0", "hg1"]
MIX = [MIX1, MIX2]
TOKEN_MAJOR = {"gv0", "gv1", "nv0", "nv1", "hi0", "hi1", "fv", "dv"}
STEPS = ["diag", 32, 16, 8, 4, 2, 1, 64, 128]
MASKED = [32, 16, 8, 4, 2, 1, 64]
SPAN_AFTER = [{i + 3: i for i in range(9)}, {i + 4: i for i in range(9)}]
ITEM_AFTER = [{4: 0, 5: 1, 6: 2, 7: 3, 8: 4, 9: 5, 10: 6, 11: 7}, {6: 0, 7: 1, 8: 2, 10: 3, 11: 4, 12: 5, 13: 6}]
ROTATE_AFTER = 9
UNITS_OUT = 4
FFN_USES = [GROUPS + 1, GROUPS, GROUPS - 1]
MIX_SLOTS = [[(i + 1) % 3 for i in range(16)], [(i + 1) % 3 for i in range(17)] + [1]]
SLOT_USES = [[2 * FFN_USES[s] + m.count(s) for s in range(3)] for m in MIX_SLOTS]
PCOLS = {"ffn1": (0, 8), "mix": (8, 8), "ffn2": (16, 8), "ogain": (24, 4), "rgain": (28, 4), "bias": (32, 4)}
PN = 36


def col_source(b, name):
    if b == 0:
        base = {"nq": 0, "nk": 512, "nv": 1024, "gq": 1536, "gk": 1792, "gv": 2048, "gr": 2560}
    else:
        base = {"fq": 0, "fk": 256, "fv": 512, "dq": 772, "dk": 1028, "dv": 1284,
                "hq": 1540, "hf": 2052, "hi": 2564, "hg": 3076}
    return base[name[:2]] + (256 * int(name[2]) if len(name) > 2 else 0)


CODE_COL, FORGET_COL = 3072, 768
OUT_PAIRS = [2, 3, 0, 1]


def build(nc, stream0, stream1, stream2, xt, params, final_gain, code_w, gate_w, forget_w, rpb,
          lower, positions, forget_bias, c_square, c_level, c_col, c_att, c_freq, c_sel, c_reset, out):
    ctx = ExitStack()
    with ctx:
        def sb(name, shape, dt=F32):
            return ctx.enter_context(nc.sbuf_tensor(name, shape, dt))

        def sem(name):
            return ctx.enter_context(nc.semaphore(name))

        streams = [stream0, stream1, stream2]
        raw = [sb(f"raw{s}", [P, RAW, UNIT]) for s in range(3)]
        w_hi = [sb(f"w_hi{s}", [P, UNIT], F32R) for s in range(3)]
        w_lo = [sb(f"w_lo{s}", [P, UNIT], F32R) for s in range(3)]
        x = sb("x", [P, KC, T])
        h = sb("h", [P, KC, T])
        h_hi = sb("h_hi", [P, KC, T], F32R)
        h_lo = sb("h_lo", [P, KC, T], F32R)
        scratch = sb("scratch", [P, 2, 512])
        act_hi = sb("act_hi", [P, 2, T], F32R)
        act_lo = sb("act_lo", [P, 2, T], F32R)
        rs = sb("rs", [P, T])
        square = sb("square", [P, 2, P])
        ident, ones = square[:, 0, :], square[:, 1, :]
        rot_m = sb("rot_m", [P, P])
        zero = sb("zero", [P, P], BF16)
        level = sb("level", [P, 2, len(MASKED), P], U8)
        reset = sb("reset", [P, T])
        cos_sin = sb("cos_sin", [P, 2, T])
        par_all = sb("par_all", [P, 2 * LAYERS, PN])
        par = sb("par", [P, PN])
        fgain = sb("fgain", [P, 2, KC])
        freq = sb("freq", [P, 1])
        eps = sb("eps", [P, 1])
        lb = sb("lb", [P, LAYERS, 4])
        lbt = sb("lbt", [P, 4, 4])
        lb_all = sb("lb_all", [P, LAYERS, 3, 4])
        lbs = sb("lbs", [P, 3, 4])
        col_mask = sb("col_mask", [P, 64])
        stat = sb("stat", [P, 2, 6])
        tot = sb("tot", [P, 4, 5])
        fbias = sb("fbias", [4, 1])

        ARENA = 15872
        arena = sb("arena", [P, ARENA])

        def part(at, *shape):
            n = 1
            for k in shape:
                n *= k
            names = "abcd"[:len(shape)]
            view = arena[:, at:at + n]
            if len(shape) == 1:
                return view
            return view.rearrange(f"p ({' '.join(names)}) -> p {' '.join(names)}",
                                  **{names[i]: shape[i] for i in range(1, len(shape))})

        aq, ak = part(0, 4, T), part(1024, 4, T)
        av = part(2048, 2, 512)
        rv = part(3072, 2, 512)
        rg = part(4096, 4, T)
        cum = part(5120, 4, T)
        dec = part(6144, 4, T)
        decay_A = part(7168, 2, 4, T)
        pT = part(9216, 2, 512)
        codes, cw = part(9216, T), part(9216 + T, KC, 32)
        qk1, qks1 = part(10240, 2, 2, T), part(11264, 2, 2, T)
        qk2, qks2 = part(10240, 2, 4, T), part(12288, 2, 4, T)
        gw = part(12288, 512)
        sig_tmp = [h[:, 4:8, :], decay_A[:, 0, :, :]]
        bias_t = part(12800, 8, 6, 64)
        att_mask = part(14336, 2, 2, T)
        fw = part(9216 + T, KC, 4)
        fc = part(15360, 2, T)[0:4]
        sel = sb("sel", [4, 4])

        bank = [ctx.enter_context(nc.psum_tensor(f"bank{i}", [P, 512], F32)) for i in range(8)]
        PB, PD, PX = bank[0:2], bank[2:6], bank[6:8]

        consts_loaded, x_loaded, small_loaded, bias_loaded = sem("consts_loaded"), sem("x_loaded"), sem("small_loaded"), sem("bias_loaded")
        mask2_loaded = sem("mask2_loaded")
        raw_ready = [sem(f"raw_ready{s}") for s in range(3)]
        hi_done = [sem(f"hi_done{s}") for s in range(3)]
        lo_done = [sem(f"lo_done{s}") for s in range(3)]
        used = [sem(f"used{s}") for s in range(3)]
        eg_ready = sem("eg_ready")
        a_ready, ahi_ready, alo_ready = sem("a_ready"), sem("ahi_ready"), sem("alo_ready")
        x_ready, sq_ready, ms_ready = sem("x_ready"), sem("sq_ready"), sem("ms_ready")
        rs_ready, h_ready, hhi_ready, hlo_ready = sem("rs_ready"), sem("h_ready"), sem("hhi_ready"), sem("hlo_ready")
        evicted = sem("evicted")
        code_ready, code_copied, z_ready, z_copied = sem("code_ready"), sem("code_copied"), sem("z_ready"), sem("z_copied")
        logit_ready, softplus_ready = sem("logit_ready"), sem("softplus_ready")
        d_ready, e_ready, qks_ready, span_ready, span_copied = sem("d_ready"), sem("e_ready"), sem("qks_ready"), sem("span_ready"), sem("span_copied")
        o_ready, o_sq, o_ms, o_rs = sem("o_ready"), sem("o_sq"), sem("o_ms"), sem("o_rs")
        mix_ready, mixhi_ready, mixlo_ready = sem("mix_ready"), sem("mixhi_ready"), sem("mixlo_ready")
        score_ready, max_ready, exp_ready, p_ready = sem("score_ready"), sem("max_ready"), sem("exp_ready"), sem("p_ready")
        pt_ready, pt_copied, head_ready, head_copied = sem("pt_ready"), sem("pt_copied"), sem("head_ready"), sem("head_copied")
        nsq, nms, nrs = sem("nsq"), sem("nms"), sem("nrs")
        rot_ready, rot_done, lb_step, ang_ready, trig_ready = sem("rot_ready"), sem("rot_done"), sem("lb_step"), sem("ang_ready"), sem("trig_ready")
        const_set, stored, bias_masked = sem("const_set"), sem("stored"), sem("bias_masked")
        layer_par = sem("layer_par")
        gsilu, rg_done = sem("gsilu"), sem("rg_done")
        heads_done = sem("heads_done")
        span_seen, load_issued = sem("span_seen"), sem("load_issued")
        forget_ready, sig_ready = sem("forget_ready"), sem("sig_ready")

        def use(b, L, s, off):
            return b * LAYERS * SLOT_USES[0][s] + L * SLOT_USES[b][s] + off

        def mix_use(b, L, i):
            s = MIX_SLOTS[b][i]
            return s, use(b, L, s, FFN_USES[s] + MIX_SLOTS[b][:i].count(s))

        def ffn_use(b, L, j, s, g):
            return use(b, L, s, g + (SLOT_USES[b][s] - FFN_USES[s] if j else 0))

        def norm_no(b, L, j):
            return 7 * b + 3 * L + j

        def split_no(b, L, j):
            return 6 * b + 3 * L + j

        def unit_no(b, L, i):
            return b * LAYERS * len(MIX1) + L * len(MIX[b]) + i

        def ffn_no(b, L, j, g):
            return (4 * b + 2 * L + j) * GROUPS + g

        def layer_no(b, L):
            return 2 * b + L

        block = ctx.enter_context(nc.Block())

        @block.sync
        def _(sp):
            def load(s, n):
                place, unit = sp.snap(n % RAW), sp.snap(n)
                sp.wait_ge(lo_done[s], n + 1)
                sp.sem_inc(load_issued, 1)
                sp.wait_ge(raw_ready[s], 16 * n + 16)
                sp.sem_inc(load_issued, 1)
                sp.dma_start(raw[s][:, bass.ds(place, 1), :], streams[s][bass.ds(unit, 1), :, :].rearrange("a p n -> p a n"))\
                    .then_inc(raw_ready[s], 16)

            def ffn(b, L, j):
                for s in range(2):
                    load(s, ffn_use(b, L, j, s, 0))
                with sp.Fori(1, GROUPS) as g:
                    for s in range(2):
                        load(s, ffn_use(b, L, j, s, g))
                    load(2, ffn_use(b, L, j, 2, g - 1))
                load(0, ffn_use(b, L, j, 0, GROUPS))

            for b in range(2):
                with sp.Fori(0, LAYERS) as L:
                    ffn(b, L, 0)
                    for i in range(len(MIX[b]) + UNITS_OUT):
                        load(*mix_use(b, L, i))
                    ffn(b, L, 1)
            sp.wait_ge(x_ready, 4 * 14 + 4)
            sp.dma_start(out, x[:, :, :]).then_inc(stored, 16)
            sp.wait_ge(stored, 16)

        @block.gpsimd
        def _(pool):
            n = [0]

            def const(dst, src):
                pool.dma_start(dst, src).then_inc(consts_loaded, 16)
                n[0] += 1

            pool.dma_start(x[:, :, :], xt).then_inc(x_loaded, 16)
            const(square[:, :, :], c_square[:, 0:2, :])
            const(rot_m[:, :], c_square[:, 2, :])
            const(part(0, 2 * len(MASKED) * P).bitcast(I32), c_level.rearrange("p a b c -> p (a b c)"))
            const(reset[:, :], c_reset)
            const(par_all[:, :, :], params)
            const(fgain[:, :, :], final_gain)
            const(freq[:, :], c_freq)
            const(lb[:, :, :], lower)
            const(col_mask[:, :], c_col)
            const(sel[:, :], c_sel)
            const(scratch[:, 0, 0:T].bitcast(I32), bass.AP(tensor=positions.tensor, offset=0, ap=[[0, P], [1, T]]))
            assert n[0] == N_CONSTS
            pool.memset(zero[:, :], 0.0).then_inc(const_set, 1)
            pool.memset(eps[:, :], EPS).then_inc(const_set, 1)
            with pool.Fori(0, LAYERS) as L:
                pool.wait_ge(heads_done, L + 1)
                pool.dma_start(cw[:, :, :], code_w[bass.ds(L, 1), :, :, :].rearrange("a p k c -> p (a k) c"))\
                    .then_inc(small_loaded, 16)
                pool.dma_start(gw[0:32, :], gate_w[bass.ds(L, 1), :, :].rearrange("a p c -> p (a c)"))\
                    .then_inc(small_loaded, 16)
                for qr in range(2):
                    for hd in range(8):
                        row = rpb[bass.ds((L * 8 + hd) * 465 + (5 - qr) * 31 - 48, 1)]
                        src = bass.AP(tensor=row.tensor, offset=row.offset, ap=[[1, 64], [31, 6], [1, 64]])
                        pool.dma_start(bias_t[64 * qr:64 * qr + 64, hd, :, :], src).then_inc(bias_loaded, 16)
                pool.wait_ge(bias_loaded, 256 * L + 256)
                flat = bias_t.rearrange("p a b c -> p (a b) c")
                pool.tensor_tensor(flat, flat, col_mask[:, None, :].to_broadcast((P, 48, 64)), ALU.add)\
                    .then_inc(bias_masked, 1)
            pool.wait_ge(heads_done, LAYERS + 1)
            pool.dma_start(att_mask[:, :, :, :], c_att).then_inc(mask2_loaded, 16)
            with pool.Fori(0, LAYERS) as L:
                pool.wait_ge(heads_done, L + LAYERS + 1)
                pool.dma_start(fw[:, :, :], forget_w[bass.ds(L, 1), :, :, :].rearrange("a p k c -> p (a k) c"))\
                    .then_inc(small_loaded, 16)
                pool.dma_start(fbias[:, :], forget_bias[bass.ds(L, 1), :, :].rearrange("a p c -> p (a c)"))\
                    .then_inc(small_loaded, 16)

        @block.tensor
        def _(pe):
            mm = nc.tensor.matmul

            def ready(s, n):
                pe.wait_ge(lo_done[s], n + RAW + 1)

            def column_unit(dst, s, token_major, first_norm=None):
                hi, lo = w_hi[s], w_lo[s]
                for c in range(2):
                    for k in range(KC):
                        if first_norm is not None and c == 0 and k % 2 == 0:
                            pe.wait_ge(hlo_ready, 4 * first_norm + k // 2 + 1)
                        o = dst[:, c * T:(c + 1) * T]
                        if token_major:
                            tok = slice(c * P, (c + 1) * P)
                            w = slice(k * 256, (k + 1) * 256)
                            trio = [(h_hi[:, k, tok], hi[:, w]), (h_hi[:, k, tok], lo[:, w]), (h_lo[:, k, tok], hi[:, w])]
                        else:
                            w = slice(k * 256 + c * P, k * 256 + (c + 1) * P)
                            trio = [(hi[:, w], h_hi[:, k, :]), (hi[:, w], h_lo[:, k, :]), (lo[:, w], h_hi[:, k, :])]
                        for j, (a, r) in enumerate(trio):
                            last = mm(o, a, r, start=(k == 0 and j == 0), stop=(k == KC - 1 and j == 2))
                return last

            def row_unit(s, chunks_hi, chunks_lo, final=False):
                for k in range(2):
                    for c in range(KC):
                        w = slice(k * D + c * P, k * D + (c + 1) * P)
                        o = PD[c // 2][:, (c % 2) * T:(c % 2 + 1) * T]
                        for j, (a, r) in enumerate(((w_hi[s], chunks_hi[:, k, :]), (w_hi[s], chunks_lo[:, k, :]), (w_lo[s], chunks_hi[:, k, :]))):
                            last = mm(o, a[:, w], r, start=False, stop=final and k == 1 and j == 2 and c % 2 == 1)
                return last

            def clear_accumulators():
                for d in PD:
                    mm(d[:, :], zero[:, :], square[:, :, :].rearrange("p a b -> p (a b)").bitcast(BF16), start=True, stop=False)

            def mean_square(nn):
                for k in range(KC):
                    if k % 2 == 0:
                        pe.wait_ge(sq_ready, 4 * nn + k // 2 + 1)
                    last = mm(PX[0][:, 0:T], ones, h[:, k, :], start=(k == 0), stop=(k == KC - 1))
                last.then_inc(ms_ready, 1)

            def ffn(b, L, j):
                nn = norm_no(b, L, 2 * j)
                mean_square(nn)
                clear_accumulators()
                n = ffn_use(b, L, j, 0, 0)
                ready(0, n)
                column_unit(PB[0], 0, False, split_no(b, L, 2 * j)).then_inc(used[0], 1)
                ready(1, ffn_use(b, L, j, 1, 0))
                column_unit(PB[1], 1, False).then_inc(used[1], 1)

                def down(g, s=2, n=None, final=False):
                    n = ffn_use(b, L, j, 2, g) if n is None else n
                    pe.wait_ge(alo_ready, ffn_no(b, L, j, g) + 1)
                    ready(s, n)
                    row_unit(s, act_hi, act_lo, final).then_inc(used[s], 1)

                with pe.Fori(1, GROUPS) as g:
                    pe.wait_ge(a_ready, ffn_no(b, L, j, g) + 1)
                    ready(0, ffn_use(b, L, j, 0, g))
                    column_unit(PB[0], 0, False).then_inc(used[0], 1)
                    ready(1, ffn_use(b, L, j, 1, g))
                    column_unit(PB[1], 1, False).then_inc(used[1], 1)
                    down(g - 1)
                down(GROUPS - 1, 0, ffn_use(b, L, j, 0, GROUPS), final=True)

            def span_step(b, L, t):
                kind = STEPS[t]
                base = len(STEPS) * layer_no(b, L) + t
                pe.wait_ge(qks_ready, base + 1)
                if t >= 1:
                    pe.wait_ge(span_copied, base)
                src = (qk1, qk2)[b] if kind == "diag" else (qks1, qks2)[b]
                for j in range(2):
                    if b == 1 and kind == 128 and j == 1:
                        continue
                    for hd in range(4):
                        if b == 0:
                            rows, ch = slice(64 * (hd % 2), 64 * (hd % 2) + 64), hd // 2
                        else:
                            rows, ch = slice(0, P), hd
                        tt = 1 - j if kind == 128 else j
                        o, at = (hd % 2, 2 * j + hd // 2) if b == 0 else (j, hd)
                        last = mm(PD[o][:, at * P:(at + 1) * P], src[rows, 1, ch, j * P:(j + 1) * P],
                                  src[rows, 0, ch, tt * P:(tt + 1) * P], start=True, stop=True)
                last.then_inc(span_ready, 1)

            def recurrence_out(b, L):
                pe.wait_ge(span_copied, len(STEPS) * (layer_no(b, L) + 1))
                for hd in range(4):
                    o = PD[hd // 2]
                    at = (hd % 2) * T
                    v0, v1 = rv[:, 0, hd * P:(hd + 1) * P], rv[:, 1, hd * P:(hd + 1) * P]
                    if b == 0:
                        mm(o[:, at:at + T], v0, decay_A[:, 0, hd, :], start=True, stop=False)
                        last = mm(o[:, at:at + T], v1, decay_A[:, 1, hd, :], start=False, stop=True)
                    else:
                        mm(o[:, at:at + P], v0, decay_A[:, 0, hd, 0:P], start=True, stop=True)
                        mm(o[:, at + P:at + T], v0, decay_A[:, 0, hd, P:T], start=True, stop=False)
                        last = mm(o[:, at + P:at + T], v1, decay_A[:, 1, hd, P:T], start=False, stop=True)
                last.then_inc(o_ready, 1)

            def recurrence_norm(b, L):
                pe.wait_ge(max_ready, 8 * layer_no(b, L) + 8)
                pe.wait_ge(o_sq, layer_no(b, L) + 1)
                for i in range(2):
                    last = mm(PX[i][:, :], ones, dec[:, 2 * i:2 * i + 2, :], start=True, stop=True)
                last.then_inc(o_ms, 1)

            def scores(b, L, i):
                hp, tile = i // 2, i % 2
                no = 8 * layer_no(b, L) + i
                if b == 1 and i == 0:
                    pe.wait_ge(forget_ready, L + 1)
                if b == 1 and i == 3:
                    pe.wait_ge(rot_done, 2 * L + 2)
                if i >= 1:
                    pe.wait_ge(max_ready, no)
                q = slice(tile * P, (tile + 1) * P)
                for e in range(2):
                    rows = slice(64 * e, 64 * e + 64)
                    fox = b == 1 and hp < 2
                    o = PX[e]
                    last = mm(o[:, 0:T], aq[rows, hp, q], ak[rows, hp, :], start=True, stop=not fox)
                    if fox:
                        hd = 2 * hp + e
                        mm(o[:, 0:T], sel[:, hd:hd + 1].to_broadcast((4, P)), fc[:, 1, :], start=False, stop=False)
                        last = mm(o[:, 0:T], fc[:, 0, q], sel[:, hd:hd + 1].to_broadcast((4, T)), start=False, stop=True)
                last.then_inc(score_ready, 1)

            def transposes(b, L, i):
                no = 8 * layer_no(b, L) + i
                pe.wait_ge(p_ready, no + 1)
                if i >= 1:
                    pe.wait_ge(pt_copied, no)
                for n in range(4):
                    last = nc.tensor.transpose(PD[2][:, n * P:(n + 1) * P], scratch[:, i % 2, n * P:(n + 1) * P], ident)
                last.then_inc(pt_ready, 1)

            def heads(b, L, i):
                hp, tile = i // 2, i % 2
                no = 8 * layer_no(b, L) + i
                pe.wait_ge(pt_copied, no + 1)
                if i >= 1:
                    pe.wait_ge(head_copied, no)
                for e in range(2):
                    for kt in range(2):
                        last = mm(PD[3][64 * e:64 * e + 64, 0:P], av[:, kt, hp * P + 64 * e:hp * P + 64 * e + 64],
                                  pT[:, i % 2, (2 * e + kt) * P:(2 * e + kt + 1) * P], start=(kt == 0), stop=(kt == 1))
                last.then_inc(head_ready, 1)

            def mixing(b, L):
                nn = norm_no(b, L, 1)
                mean_square(nn)
                width = (32, 4)[b]
                w = (cw, fw)[b]
                pe.wait_ge(small_loaded, 32 * (layer_no(b, L) + 1))
                pe.wait_ge(h_ready, 4 * split_no(b, L, 1) + 4)
                for k in range(KC):
                    last = mm(PX[1][0:width, 0:T], w[:, k, :], h[:, k, :], start=(k == 0), stop=(k == KC - 1))
                last.then_inc(code_ready, 1)
                for i, name in enumerate(MIX[b]):
                    s, n = mix_use(b, L, i)
                    ready(s, n)
                    if i >= 2:
                        pe.wait_ge(evicted, unit_no(b, L, i) - 1)
                    column_unit(PB[i % 2], s, name in TOKEN_MAJOR, split_no(b, L, 1) if i == 0 else None).then_inc(used[s], 1)
                    if b == 0 and i == 0:
                        pe.wait_ge(code_copied, L + 1)
                        for c in range(4):
                            last = mm(PD[c // 2][:, (c % 2) * T:(c % 2 + 1) * T], gw[0:32, c * P:(c + 1) * P], codes[0:32, :],
                                      start=True, stop=True)
                        last.then_inc(z_ready, 1)
                    if i in SPAN_AFTER[b]:
                        span_step(b, L, SPAN_AFTER[b][i])
                    item = ITEM_AFTER[b].get(i)
                    if item is not None:
                        before = item >= 1 and not (b == 1 and item == 3)
                        if before:
                            transposes(b, L, item - 1)
                        pe.wait_ge(evicted, unit_no(b, L, i) + 1)
                        scores(b, L, item)
                        if before:
                            heads(b, L, item - 1)
                    elif b == 1 and i == ROTATE_AFTER:
                        transposes(b, L, 2)
                        pe.wait_ge(max_ready, 8 * layer_no(b, L) + 3)
                        pe.wait_ge(evicted, unit_no(b, L, i) + 1)
                        for n in range(2):
                            mm(PX[n][:, :], rot_m[:, :], (aq, ak)[n][:, 2:4, :], start=True, stop=True).then_inc(rot_ready, 1)
                        heads(b, L, 2)
                pe.wait_ge(evicted, unit_no(b, L, len(MIX[b])))
                recurrence_out(b, L)
                if b == 1:
                    transposes(b, L, 6)
                    scores(b, L, 7)
                    heads(b, L, 6)
                recurrence_norm(b, L)
                transposes(b, L, 7)
                heads(b, L, 7)
                if b == 0:
                    pe.wait_ge(nsq, L + 1)
                    for c in range(4):
                        last = mm(PX[0][:, 0:T], ones, dec[:, c, :], start=(c == 0), stop=(c == 3))
                    last.then_inc(nms, 1)
                for i, pair in enumerate(OUT_PAIRS):
                    pe.wait_ge(mixlo_ready, 4 * layer_no(b, L) + i + 1)
                    if i == 0:
                        clear_accumulators()
                    s, n = mix_use(b, L, len(MIX[b]) + i)
                    ready(s, n)
                    row_unit(s, h_hi[:, 2 * pair:2 * pair + 2, :], h_lo[:, 2 * pair:2 * pair + 2, :], final=i == 3).then_inc(used[s], 1)

            for s in range(3):
                pe.sem_inc(used[s], 1)
            pe.wait_ge(const_set, 2)
            pe.wait_ge(consts_loaded, 16 * N_CONSTS)
            for b in range(2):
                with pe.Fori(0, LAYERS) as L:
                    ffn(b, L, 0)
                    mixing(b, L)
                    ffn(b, L, 1)
                mean_square(norm_no(b, LAYERS, 0))

        @block.scalar
        def _(act):
            fn = nc.scalar.activation

            def split(s, n):
                act.wait_ge(raw_ready[s], 16 * n + 32)
                act.wait_ge(used[s], n + 1)
                fn(w_hi[s][:, :], raw[s][:, bass.ds(n % RAW, 1), :].rearrange("p a n -> p (a n)"), ACT.Copy).then_inc(hi_done[s], 1)

            def norm(nn, sn=None):
                for k in range(4):
                    act.wait_ge(x_ready, 4 * nn + k + 1)
                    fn(h[:, 2 * k:2 * k + 2, :], x[:, 2 * k:2 * k + 2, :], ACT.Square).then_inc(sq_ready, 1)
                act.wait_ge(ms_ready, nn + 1)
                rsqrt(rs[:, :], PX[0][:, 0:T], 1.0 / D).then_inc(rs_ready, 1)
                if sn is not None:
                    for k in range(4):
                        act.wait_ge(h_ready, 4 * sn + k + 1)
                        fn(h_hi[:, 2 * k:2 * k + 2, :], h[:, 2 * k:2 * k + 2, :], ACT.Copy).then_inc(hhi_ready, 1)

            def rsqrt(dst, src, scale):
                fn(dst, src, ACT.Ln, bias=eps[:, :], scale=scale)
                act.drain()
                return fn(dst, dst, ACT.Exp, scale=-0.5)

            def ffn(b, L, j):
                nn = norm_no(b, L, 2 * j)
                for s in range(2):
                    split(s, ffn_use(b, L, j, s, 0))
                norm(nn, split_no(b, L, 2 * j))

                def gate_exp(g):
                    act.wait_ge(used[0], ffn_use(b, L, j, 0, g) + 2)
                    act.wait_ge(a_ready, ffn_no(b, L, j, g) + 1)
                    fn(scratch[:, 0, :], PB[0][:, :], ACT.Exp, scale=-1.0).then_inc(eg_ready, 1)

                def gated_hi(g):
                    act.wait_ge(a_ready, ffn_no(b, L, j, g) + 2)
                    act.wait_ge(used[2], ffn_use(b, L, j, 2, g) + 1)
                    fn(act_hi[:, :, :].rearrange("p a b -> p (a b)"), scratch[:, 1, :], ACT.Copy).then_inc(ahi_ready, 1)

                with act.Fori(1, GROUPS) as g:
                    split(0, ffn_use(b, L, j, 0, g))
                    gate_exp(g - 1)
                    split(1, ffn_use(b, L, j, 1, g))
                    gated_hi(g - 1)
                    split(2, ffn_use(b, L, j, 2, g - 1))
                split(0, ffn_use(b, L, j, 0, GROUPS))
                gate_exp(GROUPS - 1)
                gated_hi(GROUPS - 1)

            def evict(b, L, i):
                name = MIX[b][i]
                slot, n = mix_use(b, L, i)
                act.wait_ge(used[slot], n + 2)
                src = PB[i % 2][:, :]
                kind, half = name[:2], int(name[2]) if len(name) > 2 else 0
                two = src.rearrange("p (c t) -> p c t", c=2)
                pair, cols = slice(2 * half, 2 * half + 2), slice(256 * half, 256 * half + 256)
                scale = 0.125 if kind in ("nq", "gq", "fq", "dq") else 1.0
                if kind == "nq":
                    for c in range(2):
                        dst = aq[:, 2 * half + c, :]
                        rev = bass.AP(tensor=dst.tensor, offset=dst.offset + 63, ap=[dst.ap[0], [64, 4], [-1, 64]])
                        ins = fn(rev, src[:, c * T:(c + 1) * T].rearrange("p (r c) -> p r c", c=64), ACT.Copy, scale=scale)
                    ins.then_inc(evicted, 1)
                    return
                if kind in ("gr", "hq"):
                    fn(sig_tmp[b][:, pair, :], two, ACT.Exp, scale=-1.0)
                if kind == "hg":
                    fn(rg[:, pair, :], two, ACT.Exp, scale=-1.0).then_inc(evicted, 1)
                    return
                dst = {"nk": ak[:, pair, :], "gr": rg[:, pair, :], "nv": av[:, :, cols], "gv": rv[:, :, cols],
                       "hi": rv[:, :, cols], "fv": av[:, :, 0:256], "dv": av[:, :, 256:512],
                       "fq": aq[:, 0:2, :], "fk": ak[:, 0:2, :], "dq": aq[:, 2:4, :], "dk": ak[:, 2:4, :],
                       "gq": qk1[:, 0, :, :], "gk": qk1[:, 1, :, :],
                       "hq": qk2[:, 0, pair, :], "hf": qk2[:, 1, pair, :]}[kind]
                fn(dst, two, ACT.Copy, scale=scale).then_inc(evicted, 1)

            def sigmoid(t):
                act.drain()
                fn(t, t, ACT.Ln, bias=1.0)
                act.drain()
                return fn(t, t, ACT.Exp, scale=-1.0)

            def softplus(t, z, no):
                act.wait_ge(logit_ready, no + 1)
                fn(t, z, ACT.Abs)
                act.drain()
                fn(t, t, ACT.Exp, scale=-1.0)
                act.drain()
                fn(t, t, ACT.Ln, bias=1.0).then_inc(softplus_ready, 1)

            def span_exp(b, L, t):
                act.wait_ge(d_ready, (len(STEPS) - 1) * layer_no(b, L) + t)
                fn(dec[:, :, :], dec[:, :, :], ACT.Exp, scale=(1 / 16, 1.0)[b]).then_inc(e_ready, 1)

            def recurrence_squares(b, L):
                act.wait_ge(o_ready, layer_no(b, L) + 1)
                for i in range(2):
                    ins = fn(dec[:, 2 * i:2 * i + 2, :].rearrange("p a b -> p (a b)"), PD[i][:, :], ACT.Square)
                ins.then_inc(o_sq, 1)

            def recurrence_rs(b, L):
                act.wait_ge(o_ms, layer_no(b, L) + 1)
                for i in range(2):
                    fn(cum[:, 2 * i:2 * i + 2, :].rearrange("p a b -> p (a b)"), PX[i][:, :], ACT.Ln, bias=eps[:, :], scale=1.0 / P)
                act.drain()
                fn(cum[:, :, :], cum[:, :, :], ACT.Exp, scale=-0.5).then_inc(o_rs, 1)

            def mixing(b, L):
                lno = layer_no(b, L)
                nn = norm_no(b, L, 1)
                nunits = len(MIX[b])
                for i in range(3):
                    split(*mix_use(b, L, i))
                norm(nn, split_no(b, L, 1))
                act.wait_ge(code_ready, lno + 1)
                if b == 0:
                    fn(codes[0:32, :], PX[1][0:32, 0:T], ACT.Copy).then_inc(code_copied, 1)
                else:
                    softplus(scratch[0:4, 0, 0:T], fc[:, 0, :], LAYERS + 2 * L)

                def softmax(i):
                    no = 8 * lno + i
                    act.wait_ge(max_ready, no + 1)
                    for e in range(2):
                        fn(scratch[:, i % 2, e * T:(e + 1) * T], scratch[:, i % 2, e * T:(e + 1) * T], ACT.Exp,
                           bias=stat[:, i % 2, e:e + 1], accum_out=stat[:, i % 2, 2 + e:3 + e])
                    act.drain().then_inc(exp_ready, 1)

                def copy_pt(i):
                    no = 8 * lno + i
                    act.wait_ge(pt_ready, no + 1)
                    if i >= 2:
                        act.wait_ge(head_ready, no - 1)
                    fn(pT[:, i % 2, :], PD[2][:, :], ACT.Copy).then_inc(pt_copied, 1)

                def copy_head(i):
                    hp, tile = i // 2, i % 2
                    no = 8 * lno + i
                    act.wait_ge(head_ready, no + 1)
                    dst = h[:, hp, tile * P:(tile + 1) * P]
                    if b == 0:
                        rev = bass.AP(tensor=dst.tensor, offset=dst.offset + 63, ap=[dst.ap[0], [64, 2], [-1, 64]])
                        fn(rev, PD[3][:, 0:P].rearrange("p (r c) -> p r c", c=64), ACT.Copy).then_inc(head_copied, 1)
                    else:
                        fn(dst, PD[3][:, 0:P], ACT.Copy).then_inc(head_copied, 1)

                def split_mixed(k):
                    act.wait_ge(mix_ready, 4 * lno + k + 1)
                    pair = OUT_PAIRS[k]
                    fn(h_hi[:, 2 * pair:2 * pair + 2, :], h[:, 2 * pair:2 * pair + 2, :], ACT.Copy).then_inc(mixhi_ready, 1)

                for i in range(nunits):
                    evict(b, L, i)
                    split(*mix_use(b, L, i + 3))
                    if b == 0 and i == 0:
                        softplus(qks1.rearrange("p a b t -> p (a b) t"), dec[:, :, :], L)
                    if b == 1 and i == 1:
                        softplus(dec[:, :, :], qk2[:, 1, :, :], LAYERS + 2 * L + 1)
                        act.wait_ge(gsilu, L + 1)
                        fn(qk2[:, 1, :, :], qk2[:, 1, :, :], ACT.Exp)
                        fn(qks2[:, 0, :, :], qks2[:, 0, :, :], ACT.Exp)
                        act.drain()
                        fn(qks2[:, 0, :, :], qks2[:, 0, :, :], ACT.Ln, bias=1.0).then_inc(rg_done, 1)
                    if b == 1 and i == 3:
                        sigmoid(sig_tmp[1]).then_inc(sig_ready, 1)
                    item = ITEM_AFTER[b].get(i)
                    if item is not None:
                        if item >= 1 and not (b == 1 and item == 3):
                            copy_pt(item - 1)
                            copy_head(item - 1)
                        softmax(item)
                    elif b == 1 and i == ROTATE_AFTER:
                        copy_pt(2)
                        copy_head(2)
                    if i + 1 in SPAN_AFTER[b] and SPAN_AFTER[b][i + 1] == 0:
                        span_exp(b, L, 1)
                    t = SPAN_AFTER[b].get(i, 99)
                    if t + 2 < len(STEPS):
                        span_exp(b, L, t + 2)
                if b == 0:
                    sigmoid(sig_tmp[0]).then_inc(sig_ready, 1)
                else:
                    sigmoid(rg[:, :, :]).then_inc(sig_ready, 1)
                recurrence_squares(b, L)
                if b == 1:
                    copy_pt(6)
                    copy_head(6)
                    softmax(7)
                recurrence_rs(b, L)
                copy_pt(7)
                copy_head(7)
                for k in range(2):
                    split_mixed(k)
                if b == 0:
                    act.drain()
                    fn(dec[:, :, :], h[:, 0:4, :], ACT.Square).then_inc(nsq, 1)
                    act.wait_ge(nms, L + 1)
                    rsqrt(rs[:, :], PX[0][:, 0:T], 1.0 / 512).then_inc(nrs, 1)
                for k in range(2, 4):
                    split_mixed(k)
                split(*mix_use(b, L, nunits + 3))

            act.wait_ge(ang_ready, 1)
            fn(cos_sin[:, :, :], cos_sin[:, :, :], ACT.Sin).then_inc(trig_ready, 1)
            act.add_instruction(mybir.InstLoadActFuncSet(name=nc.get_next_instruction_name(), act_func_set_id=EXP_LN_SET, ins=[], outs=[]))
            act.wait_ge(lb_step, 1)
            fn(lbt[:, 0:2, :], lbt[:, 0:2, :], ACT.Exp).then_inc(lb_step, 1)
            act.wait_ge(lb_step, 3)
            fn(lb_all[:, :, 0, :], lb_all[:, :, 0, :], ACT.Ln, scale=2.0 ** 40)
            fn(lb_all[:, :, 1, :], lb_all[:, :, 2, :], ACT.Ln).then_inc(lb_step, 1)
            for b in range(2):
                with act.Fori(0, LAYERS) as L:
                    ffn(b, L, 0)
                    mixing(b, L)
                    ffn(b, L, 1)
                norm(norm_no(b, LAYERS, 0))

        @block.vector
        def _(dve):
            v = nc.vector
            tt, ts, stt = v.tensor_tensor, v.tensor_scalar, v.scalar_tensor_tensor

            def wide(ap, *shape):
                return ap.to_broadcast(shape)

            def split(s, n):
                dve.wait_ge(hi_done[s], n + 1)
                tt(w_lo[s][:, :], raw[s][:, bass.ds(n % RAW, 1), :].rearrange("p a n -> p (a n)"), w_hi[s][:, :].bitcast(F32),
                   ALU.subtract).then_inc(lo_done[s], 1)

            def gain(col, k):
                return par[:, PCOLS[col][0] + k:PCOLS[col][0] + k + 1]

            def norm(nn, sn, col):
                dve.wait_ge(rs_ready, nn + 1)
                for k in range(KC):
                    ins = stt(h[:, k, :], x[:, k, :], gain(col, k), rs[:, :], ALU.mult, ALU.mult)
                    if k % 2:
                        ins.then_inc(h_ready, 1)
                for k in range(4):
                    dve.wait_ge(hhi_ready, 4 * sn + k + 1)
                    two = slice(2 * k, 2 * k + 2)
                    tt(h_lo[:, two, :], h[:, two, :], h_hi[:, two, :].bitcast(F32), ALU.subtract).then_inc(hlo_ready, 1)

            def update(s, n, scale):
                dve.wait_ge(used[s], n + 2)
                for k in range(4):
                    two = x[:, 2 * k:2 * k + 2, :].rearrange("p a b -> p (a b)")
                    stt(two, PD[k][:, :], scale, two, ALU.mult, ALU.add).then_inc(x_ready, 1)

            def ffn(b, L, j):
                nn = norm_no(b, L, 2 * j)
                for s in range(2):
                    split(s, ffn_use(b, L, j, s, 0))
                norm(nn, split_no(b, L, 2 * j), ("ffn1", "ffn2")[j])

                def gated(g):
                    dve.wait_ge(eg_ready, ffn_no(b, L, j, g) + 1)
                    e = scratch[:, 0, :]
                    ts(e, e, 1.0, None, ALU.add)
                    dve.drain()
                    v.reciprocal(e, e)
                    dve.drain()
                    tt(e, e, PB[0][:, :], ALU.mult)
                    dve.drain()
                    dve.wait_ge(used[1], ffn_use(b, L, j, 1, g) + 2)
                    tt(scratch[:, 1, :], e, PB[1][:, :], ALU.mult).then_inc(a_ready, 1)

                def gated_lo(g):
                    dve.wait_ge(ahi_ready, ffn_no(b, L, j, g) + 1)
                    tt(act_lo[:, :, :].rearrange("p a b -> p (a b)"), scratch[:, 1, :],
                       act_hi[:, :, :].rearrange("p a b -> p (a b)").bitcast(F32), ALU.subtract).then_inc(alo_ready, 1)

                with dve.Fori(1, GROUPS) as g:
                    split(0, ffn_use(b, L, j, 0, g))
                    gated(g - 1)
                    split(1, ffn_use(b, L, j, 1, g))
                    gated_lo(g - 1)
                    split(2, ffn_use(b, L, j, 2, g - 1))
                split(0, ffn_use(b, L, j, 0, GROUPS))
                gated(GROUPS - 1)
                gated_lo(GROUPS - 1)
                update(0, ffn_use(b, L, j, 0, GROUPS), 0.5)

            def halves(ap, m):
                w = ap.rearrange("p c (n two m) -> p (c n) two m", two=2, m=m)
                return w[:, :, 0, :], w[:, :, 1, :]

            def less(dst, a, r):
                shape = tuple(dst.shape)
                a = a if tuple(a.shape) == shape else wide(a, *shape)
                r = r if tuple(r.shape) == shape else wide(r, *shape)
                return tt(dst, a, r, ALU.subtract)

            def chunk(ap, c):
                return ap[:, :, 64 * c:64 * c + 64]

            def span_decay(b, L, t):
                m = STEPS[t]
                fq, fk = (dec[:, 0:2, :], dec[:, 2:4, :]) if b == 0 else (dec[:, :, :], dec[:, :, :])
                fx, ft = (cum[:, 0:2, :], tot[:, 0:2, :]) if b == 0 else (cum[:, :, :], tot[:, :, :])
                bx, bt = cum[:, 2:4, :], tot[:, 2:4, :]
                if m <= 32:
                    (lo, up) = halves(fx, m)
                    ref = lo[:, :, m - 1:m]
                    less(halves(fq, m)[1], up, ref)
                    ins = less(halves(fk, m)[0], ref, lo)
                    if b == 0:
                        lo, up = halves(bx, m)
                        ref = up[:, :, 0:1]
                        less(halves(fq, m)[0], ref, lo)
                        ins = less(halves(fk, m)[1], up, ref)
                elif m == 64:
                    for a in range(2):
                        v.tensor_copy(chunk(fq, 2 * a + 1), chunk(fx, 2 * a + 1))
                        ins = less(chunk(fk, 2 * a), ft[:, :, 2 * a:2 * a + 1], chunk(fx, 2 * a))
                        if b == 0:
                            less(chunk(fq, 2 * a), bt[:, :, 2 * a:2 * a + 1], chunk(bx, 2 * a))
                            ins = v.tensor_copy(chunk(fk, 2 * a + 1), chunk(bx, 2 * a + 1))
                else:
                    def add(dst, a, r):
                        return tt(dst, a, wide(r, *dst.shape), ALU.add)
                    v.tensor_copy(chunk(fq, 2), chunk(fx, 2))
                    add(chunk(fq, 3), chunk(fx, 3), ft[:, :, 2:3])
                    less(chunk(fk, 1), ft[:, :, 1:2], chunk(fx, 1))
                    ins = less(chunk(fk, 0), ft[:, :, 4:5], chunk(fx, 0))
                    if b == 0:
                        less(chunk(fq, 1), bt[:, :, 1:2], chunk(bx, 1))
                        less(chunk(fq, 0), bt[:, :, 4:5], chunk(bx, 0))
                        v.tensor_copy(chunk(fk, 2), chunk(bx, 2))
                        ins = add(chunk(fk, 3), chunk(bx, 3), bt[:, :, 2:3])
                ins.then_inc(d_ready, 1)

            def span_scale(b, L, t):
                no = len(STEPS) * layer_no(b, L) + t
                if t == 0:
                    dve.sem_inc(qks_ready, 1)
                    return
                dve.wait_ge(e_ready, (len(STEPS) - 1) * layer_no(b, L) + t)
                if b == 0:
                    tt(qks1.rearrange("p a b t -> p (a b t)"), qk1.rearrange("p a b t -> p (a b t)"),
                       dec[:, :, :].rearrange("p a t -> p (a t)"), ALU.mult).then_inc(qks_ready, 1)
                else:
                    m = STEPS[t]
                    tt(halves(qks2[:, 0, :, :], m)[1], halves(qk2[:, 0, :, :], m)[1], halves(dec[:, :, :], m)[1], ALU.mult)
                    tt(halves(qks2[:, 1, :, :], m)[0], halves(qk2[:, 1, :, :], m)[0], halves(dec[:, :, :], m)[0], ALU.mult)\
                        .then_inc(qks_ready, 1)

            def span_copy(b, L, t):
                kind = STEPS[t]
                no = len(STEPS) * layer_no(b, L) + t
                dve.wait_ge(span_ready, no + 1)
                dve.sem_inc(span_seen, 1)
                for n in range(2):
                    if b == 1 and kind == 128 and n == 1:
                        continue
                    if b == 0:
                        swap = kind == 128
                        base = decay_A[:, 0, n, P if swap else 0:T]
                        dst = bass.AP(tensor=base.tensor, offset=base.offset,
                                      ap=[base.ap[0], [4 * T - P if swap else 4 * T + P, 2], [2 * T, 2], [1, P]])
                        src = PD[n][:, :].rearrange("p (j h t) -> p j h t", j=2, h=2)
                        spread = lambda m: wide(m[:, None, None, :], P, 2, 2, P)
                    else:
                        tile = 1 - n if kind == 128 else n
                        dst = decay_A[:, n, :, tile * P:(tile + 1) * P]
                        src = PD[n][:, :].rearrange("p (h t) -> p h t", h=4)
                        spread = lambda m: wide(m[:, None, :], P, 4, P)
                    if kind == "diag":
                        ins = tt(dst, src, spread(ident), ALU.mult)
                    elif kind == 128:
                        ins = v.tensor_copy(dst, src)
                    else:
                        ins = v.copy_predicated(dst, spread(level[:, b, MASKED.index(kind), :]), src)
                ins.then_inc(span_copied, 1)
                dve.drain()

            def scans(rows, src, dst):
                for c in range(4):
                    v.tensor_tensor_scan(dst[:, c, :], reset[:, :], src[:, c, :], 0.0, ALU.mult, ALU.add)
                dve.drain()
                v.tensor_copy(tot[:, :, 0:4], dst.rearrange("p c (n t) -> p c n t", t=64)[:, :, :, 63])
                dve.drain()
                tt(tot[:, :, 4:5], tot[:, :, 0:1], tot[:, :, 1:2], ALU.add)

            def gates(b, L):
                tmp = qks1.rearrange("p a b t -> p (a b) t")
                dve.wait_ge(z_ready, L + 1)
                for c in range(4):
                    ts(dec[:, c, :], PD[c // 2][:, (c % 2) * T:(c % 2 + 1) * T], gain("bias", c), None, ALU.add)
                dve.drain().then_inc(logit_ready, 1)
                dve.wait_ge(softplus_ready, L + 1)
                stt(dec[:, :, :], dec[:, :, :], 0.0, tmp, ALU.min, ALU.subtract)
                dve.drain()
                scans(4, dec, cum)
                tt(cum[:, 2:4, :], cum[:, 2:4, :], dec[:, 2:4, :], ALU.subtract)
                dve.drain()

            def forget_sums(L):
                z, t = fc[:, 0, :], scratch[0:4, 0, 0:T]
                dve.wait_ge(code_ready, LAYERS + L + 1)
                dve.wait_ge(small_loaded, 32 * (LAYERS + L + 1))
                v.memset(fc[:, 1, :], 1.0)
                ts(z, PX[1][0:4, 0:T], fbias[:, :], None, ALU.add).then_inc(logit_ready, 1)
                dve.wait_ge(softplus_ready, LAYERS + 2 * L + 1)
                stt(z, z, 0.0, t, ALU.min, ALU.subtract)
                dve.drain()
                v.tensor_tensor_scan(t, fc[:, 1, :], z, 0.0, ALU.mult, ALU.add)
                dve.drain()
                ts(fc[:, 0, :], t, 1.0, None, ALU.mult)
                ts(fc[:, 1, :], t, -1.0, None, ALU.mult)
                dve.drain().then_inc(forget_ready, 1)

            def hgrn_gates(L):
                z, mx, mn = qk2[:, 1, :, :], qks2[:, 1, :, :], qks2[:, 0, :, :]
                dve.wait_ge(evicted, unit_no(1, L, 1) + 1)
                dve.sem_inc(logit_ready, 1)
                dve.wait_ge(softplus_ready, LAYERS + 2 * L + 2)
                stt(dec[:, :, :], z, 0.0, dec[:, :, :], ALU.min, ALU.subtract)
                dve.drain()
                tt(z, dec[:, :, :], z, ALU.subtract)
                tt(dec[:, :, :], dec[:, :, :], wide(lbs[:, 1, :, None], P, 4, T), ALU.add)
                dve.drain()
                tt(mx, dec[:, :, :], wide(lbs[:, 0, :, None], P, 4, T), ALU.max)
                tt(mn, dec[:, :, :], wide(lbs[:, 0, :, None], P, 4, T), ALU.min)
                dve.drain()
                tt(mn, mn, mx, ALU.subtract).then_inc(gsilu, 1)
                dve.wait_ge(rg_done, L + 1)
                tt(mx, mx, mn, ALU.add)
                tt(z, z, wide(lbs[:, 2, :, None], P, 4, T), ALU.mult)
                dve.drain()
                scans(4, mx, cum)
                dve.drain()

            def recurrence_out(b, L):
                lno = layer_no(b, L)
                dve.wait_ge(sig_ready, L + 1 if b == 0 else 2 * L + 4)
                if b == 0:
                    tt(rg[:, :, :], rg[:, :, :], sig_tmp[0], ALU.mult)
                    dve.drain()
                else:
                    dve.sem_inc(span_seen, 1)
                dve.wait_ge(o_rs, lno + 1)
                for hd in range(4):
                    stt(h[:, 4 + hd, :], PD[hd // 2][:, (hd % 2) * T:(hd % 2 + 1) * T], gain("rgain", hd), cum[:, hd, :],
                        ALU.mult, ALU.mult)
                dve.drain()
                for k in range(2):
                    tt(h[:, 4 + 2 * k:6 + 2 * k, :], h[:, 4 + 2 * k:6 + 2 * k, :], rg[:, 2 * k:2 * k + 2, :], ALU.mult)\
                        .then_inc(mix_ready, 1)

            def mixed_lo(lno, k):
                dve.wait_ge(mixhi_ready, 4 * lno + k + 1)
                two = slice(2 * OUT_PAIRS[k], 2 * OUT_PAIRS[k] + 2)
                tt(h_lo[:, two, :], h[:, two, :], h_hi[:, two, :].bitcast(F32), ALU.subtract).then_inc(mixlo_ready, 1)

            def mixing(b, L):
                lno = layer_no(b, L)
                nunits = len(MIX[b])
                for i in range(3):
                    split(*mix_use(b, L, i))
                norm(norm_no(b, L, 1), split_no(b, L, 1), "mix")
                def rotate(L):
                    for i in range(2):
                        dve.wait_ge(rot_ready, 2 * L + i + 1)
                        y, t = (aq, ak)[i][:, 2:4, :], scratch[:, 1, :].rearrange("p (c t) -> p c t", c=2)
                        tt(t, PX[i][:, :].rearrange("p (c t) -> p c t", c=2), wide(cos_sin[:, 1:2, :], P, 2, T), ALU.mult)
                        tt(y, y, wide(cos_sin[:, 0:1, :], P, 2, T), ALU.mult)
                        dve.drain()
                        tt(y, y, t, ALU.add).then_inc(rot_done, 1)
                        dve.drain()

                def masked(i):
                    hp, tile = i // 2, i % 2
                    no = 8 * lno + i
                    dve.wait_ge(score_ready, no + 1)
                    sc = scratch[:, i % 2, :].rearrange("p (e k) -> p e k", e=2)
                    if i >= 2:
                        dve.wait_ge(pt_ready, no - 1)
                    for e in range(2):
                        if b == 0:
                            extra = bias_t[:, 2 * hp + e, 2 - 2 * tile:6 - 2 * tile, :].rearrange("p r c -> p (r c)")
                        else:
                            extra = att_mask[:, hp // 2, tile, :]
                        tt(sc[:, e, :], PX[e][:, 0:T], extra, ALU.add)
                    dve.drain()
                    v.tensor_reduce(stat[:, i % 2, 4:6], sc, AX.X, ALU.max)
                    dve.drain()
                    ts(stat[:, i % 2, 0:2], stat[:, i % 2, 4:6], -1.0, None, ALU.mult).then_inc(max_ready, 1)

                def normalise(i):
                    no = 8 * lno + i
                    dve.wait_ge(exp_ready, no + 1)
                    v.reciprocal(stat[:, i % 2, 2:4], stat[:, i % 2, 2:4])
                    dve.drain()
                    for e in range(2):
                        sc = scratch[:, i % 2, e * T:(e + 1) * T]
                        ins = ts(sc, sc, stat[:, i % 2, 2 + e:3 + e], None, ALU.mult)
                    ins.then_inc(p_ready, 1)

                if b == 1:
                    forget_sums(L)
                for i in range(nunits):
                    split(*mix_use(b, L, i + 3))
                    if b == 0 and i == 0:
                        gates(b, L)
                    if b == 1 and i == 1:
                        hgrn_gates(L)
                    if b == 1 and i == 3:
                        dve.wait_ge(sig_ready, 2 * L + 3)
                        tt(qk2[:, 0, :, :], qk2[:, 0, :, :], sig_tmp[1], ALU.mult)
                        dve.drain()
                    t = SPAN_AFTER[b].get(i, 99)
                    if i + 1 in SPAN_AFTER[b] and SPAN_AFTER[b][i + 1] == 0:
                        dve.wait_ge(evicted, unit_no(b, L, (1, 3)[b]) + 1)
                        span_scale(b, L, 0)
                        span_decay(b, L, 1)
                    if t < len(STEPS):
                        span_copy(b, L, t)
                    item = ITEM_AFTER[b].get(i)
                    if item is not None:
                        if item == 0:
                            if b == 0:
                                dve.wait_ge(bias_masked, L + 1)
                            else:
                                dve.wait_ge(mask2_loaded, 16)
                        masked(item)
                    elif b == 1 and i == ROTATE_AFTER:
                        rotate(L)
                    if t + 1 < len(STEPS):
                        span_scale(b, L, t + 1)
                    if t + 2 < len(STEPS):
                        dve.drain()
                        span_decay(b, L, t + 2)
                    if item is not None:
                        normalise(item)
                if b == 1:
                    masked(7)
                    normalise(7)
                recurrence_out(b, L)
                mixed_lo(lno, 0)
                mixed_lo(lno, 1)
                if b == 0:
                    dve.wait_ge(nrs, L + 1)
                    for k in range(2):
                        for c in range(2 * k, 2 * k + 2):
                            ins = stt(h[:, c, :], h[:, c, :], gain("ogain", c), rs[:, :], ALU.mult, ALU.mult)
                        ins.then_inc(mix_ready, 1)
                else:
                    dve.wait_ge(head_copied, 8 * lno + 8)
                    dve.sem_inc(mix_ready, 2)
                mixed_lo(lno, 2)
                mixed_lo(lno, 3)
                dve.drain().then_inc(heads_done, 1)
                split(*mix_use(b, L, nunits + 3))
                update(*mix_use(b, L, nunits + 3), 1.0)

            for s in range(3):
                dve.sem_inc(lo_done[s], RAW)
                dve.sem_inc(raw_ready[s], 16)
            dve.sem_inc(a_ready, 1)
            dve.sem_inc(heads_done, 1)
            dve.wait_ge(consts_loaded, 16 * N_CONSTS)
            v.tensor_copy(level[:, :, :, :].rearrange("p a b c -> p (a b c)"), part(0, 2 * len(MASKED) * P).bitcast(I32))
            posf, ang, turns = scratch[:, 0, T:2 * T], scratch[:, 1, 0:T], scratch[:, 1, T:2 * T]
            v.tensor_copy(posf, scratch[:, 0, 0:T].bitcast(I32))
            dve.drain()
            ts(ang, posf, freq[:, :], None, ALU.mult)
            dve.drain()
            ts(turns, ang, 1.0 / (2 * np.pi), None, ALU.mult)
            dve.drain()
            ts(turns, turns, ROUND, None, ALU.add)
            dve.drain()
            ts(turns, turns, ROUND, None, ALU.subtract)
            dve.drain()
            for piece in TWO_PI:
                stt(ang, turns, -piece, ang, ALU.mult, ALU.add)
                dve.drain()
            ts(posf, ang, float(np.pi / 2), None, ALU.is_gt)
            dve.drain()
            stt(posf, posf, float(-2 * np.pi), ang, ALU.mult, ALU.add)
            dve.drain()
            ts(posf, posf, float(np.pi / 2), None, ALU.add)
            dve.drain()
            for i, a in enumerate((posf, ang)):
                ins = ts(cos_sin[:, i, :], a, PI_IN, -PI_IN, ALU.min, ALU.max)
            ins.then_inc(ang_ready, 1)
            tt(lbt[:, 2, :], lb[:, 0, :], lb[:, 1, :], ALU.max)
            dve.drain()
            tt(lbt[:, 0:2, :], lb[:, :, :], wide(lbt[:, 2:3, :], P, 2, 4), ALU.subtract).then_inc(lb_step, 1)
            dve.wait_ge(lb_step, 2)
            tt(lbt[:, 2, :], lbt[:, 0, :], lbt[:, 1, :], ALU.add)
            dve.drain()
            v.reciprocal(lbt[:, 3, :], lbt[:, 2, :])
            dve.drain()
            tt(lbt[:, 0:2, :], lbt[:, 0:2, :], wide(lbt[:, 3:4, :], P, 2, 4), ALU.mult)
            dve.drain()
            tt(lbt[:, 2, :], lbt[:, 0, :], lbt[:, 1, :], ALU.add)
            dve.drain()
            tt(lb[:, 0, :], lbt[:, 0, :], lbt[:, 0, :], ALU.subtract)
            tt(lb[:, 1, :], lbt[:, 2, :], lbt[:, 0, :], ALU.subtract)
            dve.drain()
            ts(lb[:, :, :], lb[:, :, :], 0.0, 1.0 - 1e-6, ALU.max, ALU.min)
            dve.drain()
            ts(lb_all[:, :, 2, :], lb[:, :, :], -1.0, 1.0, ALU.mult, ALU.add)
            ts(lb_all[:, :, 0, :], lb[:, :, :], 1e-30, None, ALU.max).then_inc(lb_step, 1)
            dve.wait_ge(lb_step, 4)
            ts(lb_all[:, :, 0, :], lb_all[:, :, 0, :], float(40 * np.log(2.0)), None, ALU.subtract)
            dve.wait_ge(trig_ready, 1)
            dve.wait_ge(x_loaded, 16)
            dve.sem_inc(x_ready, 4)
            for b in range(2):
                with dve.Fori(0, LAYERS) as L:
                    v.tensor_copy(par[:, :], par_all[:, bass.ds(layer_no(b, L), 1), :].rearrange("p a n -> p (a n)"))
                    if b == 1:
                        v.tensor_copy(lbs[:, :, :].rearrange("p a b -> p (a b)"),
                                      lb_all[:, bass.ds(L, 1), :, :].rearrange("p a b c -> p (a b c)"))
                    dve.drain()
                    ffn(b, L, 0)
                    mixing(b, L)
                    ffn(b, L, 1)
                nn = norm_no(b, LAYERS, 0)
                dve.wait_ge(rs_ready, nn + 1)
                for k in range(KC):
                    ins = stt(x[:, k, :], x[:, k, :], fgain[:, b, k:k + 1], rs[:, :], ALU.mult, ALU.mult)
                    if k % 2:
                        ins.then_inc(x_ready, 1)
                dve.drain()


N_CONSTS = 11
ROUND = 1.5 * 2.0 ** 23
TWO_PI = [6.28125, 0.0019350051879882812, float(2 * np.pi - 6.28125 - 0.0019350051879882812)]
PI_IN = float(np.nextafter(np.float32(np.pi), np.float32(0)))


def constants():
    c = {}
    sq = np.zeros((P, 3, P), np.float32)
    sq[:, 0] = np.eye(P)
    sq[:, 1] = 1.0
    for i in range(P):
        j = i % 64
        if j < 8:
            sq[i + 8, 2, i] = -1.0
        elif j < 16:
            sq[i - 8, 2, i] = 1.0
    c["c_square"] = sq
    s, t = np.arange(P)[:, None], np.arange(P)[None, :]
    lv = np.zeros((P, 2, len(MASKED), P), np.int32)
    for i, m in enumerate(MASKED):
        same = s // (2 * m) == t // (2 * m)
        forward = same & (s // m % 2 == 0) & (t // m % 2 == 1)
        backward = same & (s // m % 2 == 1) & (t // m % 2 == 0)
        lv[:, 0, i] = forward | backward
        lv[:, 1, i] = forward
    c["c_level"] = lv
    qc = 63 - np.arange(P)[:, None] % 64
    kc = np.arange(64)[None, :]
    start = np.clip(qc - 8, 0, 48)
    c["c_col"] = np.where((kc >= start) & (kc < start + 16), 0.0, NEG).astype(np.float32)
    am = np.full((P, 2, 2, T), NEG, np.float32)
    for tile in range(2):
        q = tile * P + np.arange(P)[:, None]
        k = np.arange(T)[None, :]
        rel = q - k
        am[:, 0, tile] = np.where(rel >= 0, 0.0, NEG)
        times = (((rel >= 0) & (rel <= 128)).astype(int) + ((rel >= 0) & (rel % 4 == 0) & (rel <= 512))
                 + ((rel >= 0) & (rel % 16 == 0) & (rel <= 2048)))
        am[:, 1, tile] = np.where(times > 0, np.log(np.maximum(times, 1)), NEG)
    c["c_att"] = am
    f = 500000.0 ** (-np.arange(0, 16, 2, dtype=np.float32) / np.float32(16))
    j = np.arange(P) % 64
    c["c_freq"] = np.where(j < 16, f[j % 8], 0.0).astype(np.float32)[:, None]
    c["c_sel"] = np.eye(4, dtype=np.float32)
    c["c_reset"] = np.broadcast_to((np.arange(T) % 64 != 0).astype(np.float32), (P, T)).copy()
    return c


def column_layout(w, c, n=256):
    return w[:, c:c + n].reshape(KC, P, n).transpose(1, 0, 2)


def weight_streams(i):
    out = [[], [], []]
    names = [("ffn1_wg", "ffn1_wu", "ffn1_wd", "w_in", "w_out", "ffn2_wg", "ffn2_wu", "ffn2_wd"),
             ("ffn1_w_gate_2", "ffn1_w_up_2", "ffn1_w_down_2", "w_in_2", "w_out_2",
              "ffn2_w_gate_2", "ffn2_w_up_2", "ffn2_w_down_2")]
    for b in range(2):
        g1, u1, d1, w_in, w_out, g2, u2, d2 = (i[k] for k in names[b])
        for L in range(LAYERS):
            def ffn(g, u, d):
                for n in range(GROUPS):
                    out[0].append(column_layout(g[L], 256 * n).reshape(P, UNIT))
                    out[1].append(column_layout(u[L], 256 * n).reshape(P, UNIT))
                    out[2 if n < GROUPS - 1 else 0].append(
                        d[L][256 * n:256 * n + 256].reshape(2, P, D).transpose(1, 0, 2).reshape(P, UNIT))
            ffn(g1, u1, d1)
            for n, name in enumerate(MIX[b]):
                out[MIX_SLOTS[b][n]].append(column_layout(w_in[L], col_source(b, name)).reshape(P, UNIT))
            for n, pair in enumerate(OUT_PAIRS):
                out[MIX_SLOTS[b][len(MIX[b]) + n]].append(w_out[L][256 * pair:256 * pair + 256].reshape(2, P, D).transpose(1, 0, 2).reshape(P, UNIT))
            ffn(g2, u2, d2)
    return [np.stack(o) for o in out]


def kernel(**inputs):
    import concourse.bacc as bacc
    from concourse.bass_utils import run_bass_kernel_spmd

    i = {k: np.asarray(v) for k, v in inputs.items()}

    def per_part(v):
        return v.reshape(-1, P).T

    arrays = {}
    for s, a in enumerate(weight_streams(i)):
        arrays[f"stream{s}"] = a
    arrays["xt"] = np.ascontiguousarray(i["x"][0].T.reshape(KC, P, T).transpose(1, 0, 2))
    pars = []
    for b, tail in enumerate(("", "_2")):
        for L in range(LAYERS):
            cols = [per_part(i[n + tail][L]) for n in ("ffn1_norm", "mix_norm", "ffn2_norm")]
            if b == 0:
                cols += [per_part(i["na_gain"][L])] + [per_part(i["gla_gain"][L])] * 4
                cols += [per_part(i["b_gate_f"][L]), per_part(i["b_gate_b"][L])]
            else:
                cols += [per_part(i["hgrn_out_norm_2"][L])] * 2 + [per_part(i["hgrn_out_norm_2"][L])]
            pars.append(np.concatenate(cols, 1))
    arrays["params"] = np.ascontiguousarray(np.stack(pars, 1))
    arrays["final_gain"] = np.ascontiguousarray(np.stack([per_part(i["final_norm"]), per_part(i["final_norm_2"])], 1))
    arrays["code_w"] = np.ascontiguousarray(np.stack([column_layout(i["w_in"][L], CODE_COL, 32) for L in range(LAYERS)]))
    gate_w = np.zeros((LAYERS, 32, 512), np.float32)
    gate_w[:, 0:16, 0:256] = i["w_gate_f"]
    gate_w[:, 16:32, 256:512] = i["w_gate_b"]
    arrays["gate_w"] = gate_w
    arrays["forget_w"] = np.ascontiguousarray(np.stack([column_layout(i["w_in_2"][L], FORGET_COL, 4) for L in range(LAYERS)]))
    arrays["rpb"] = np.ascontiguousarray(i["na_rpb"].reshape(-1))
    arrays["lower"] = np.ascontiguousarray(np.stack([per_part(i["hgrn_lower_bounds_2"][L]) for L in range(LAYERS)], 1))
    arrays["positions"] = np.ascontiguousarray(i["positions_2"].reshape(1, T))
    arrays["forget_bias"] = np.ascontiguousarray(i["fox_forget_bias_2"].reshape(LAYERS, 4, 1))
    arrays.update(constants())

    nc = bacc.Bacc("TRN2", target_bir_lowering=False, num_devices=1)
    args = [nc.dram_tensor(n, a.shape, mybir.dt.from_np(a.dtype), kind="ExternalInput").ap() for n, a in arrays.items()]
    out = nc.dram_tensor("out", (P, KC, T), F32, kind="ExternalOutput").ap()
    build(nc, *args, out)
    r = run_bass_kernel_spmd(nc, [arrays], core_ids=[0]).results[0]["out"]
    return np.ascontiguousarray(r.transpose(1, 0, 2).reshape(D, T).T)[None]
```
